# Optimizing a Trainium2 kernel written in Bass

```python
import math, functools
import jax, jax.numpy as jnp
from jax import lax
import numpy as np

D_MODEL = 1024
BATCH = 1
SEQ = 256
DEPTH = 1
DEC_BATCH = 8
DEC_SEQ = 1
PAST_LEN = 2048
PAGE_SIZE = 128

RET_HEADS = 4
RET_DK = 128
RET_DV = 256
RET_QK_W = RET_HEADS * RET_DK
RET_V_W = RET_HEADS * RET_DV
RET_CHUNK = 128
ROPE_BASE = 10000.0
GDN_HEADS = 8
GDN_DK = 128
GDN_DV = 128
GDN_QK_W = GDN_HEADS * GDN_DK
GDN_V_W = GDN_HEADS * GDN_DV
GDN_CHUNK = 64
CONV_W = 4
CONV_CH = 2 * GDN_QK_W + GDN_V_W
IN_SPLITS = (RET_QK_W, RET_QK_W, RET_V_W, RET_V_W, CONV_CH, GDN_V_W, GDN_HEADS, GDN_HEADS, D_MODEL, D_MODEL)
IN_WIDTH = sum(IN_SPLITS)
N_EXPERTS = 32
TOP_K = 4
D_FF = D_MODEL
SWIGLU_LIMIT = 7.0
SWIGLU_ALPHA = 1.702
MOE_BLOCK = 128
NORM_EPS = 1e-6

kernel_name = "hybrid_retention_gdn_moe_step"

def rms_normalize(x):
    xf = x.astype(jnp.float32)
    return xf * lax.rsqrt(jnp.mean(xf * xf, axis=-1, keepdims=True) + NORM_EPS)

def rmsnorm(x, w):
    return (rms_normalize(x) * w.astype(jnp.float32)).astype(x.dtype)

def l2norm(x):
    return x * lax.rsqrt(jnp.sum(x * x, axis=-1, keepdims=True) + NORM_EPS)

def rotary(x, pos):
    half = x.shape[-1] // 2
    inv = 1.0 / (ROPE_BASE ** (jnp.arange(half, dtype=jnp.float32) / half))
    ang = pos.astype(jnp.float32)[:, None] * inv[None, :]
    cos = jnp.cos(ang)[None, :, None, :]
    sin = jnp.sin(ang)[None, :, None, :]
    x1, x2 = x[..., :half], x[..., half:]
    return jnp.concatenate([x1 * cos - x2 * sin, x1 * sin + x2 * cos], axis=-1)

def chunk_scan(step, s0, seqs, chunk):
    B, H, L = seqs[0].shape[:3]
    c = chunk if L % chunk == 0 else L
    n = L // c
    xs = tuple(jnp.moveaxis(a.reshape((B, H, n, c) + a.shape[3:]), 2, 0) for a in seqs)
    s, ys = lax.scan(step, s0, xs)
    ys = jnp.moveaxis(ys, 0, 2)
    return s, ys.reshape((B, H, L) + ys.shape[4:])

def retention_step(lg, S, xs):
    q, k, v = xs
    c = q.shape[2]
    idx = jnp.arange(c, dtype=jnp.float32)
    diff = idx[:, None] - idx[None, :]
    causal = diff >= 0
    dmask = jnp.where(causal[None], jnp.exp(jnp.where(causal, diff, 0.0)[None] * lg[:, None, None]), 0.0)
    inner = jnp.einsum('bhid,bhjd->bhij', q, k) * dmask[None]
    q_dec = q * jnp.exp((idx + 1.0)[None, :] * lg[:, None])[None, :, :, None]
    o = jnp.einsum('bhij,bhje->bhie', inner, v) + jnp.einsum('bhid,bhde->bhie', q_dec, S)
    k_dec = k * jnp.exp((c - 1.0 - idx)[None, :] * lg[:, None])[None, :, :, None]
    S_new = S * jnp.exp(c * lg)[None, :, None, None] + jnp.einsum('bhjd,bhje->bhde', k_dec, v)
    return S_new, o

def gdn_step(S, xs):
    q, k, v, g, beta = xs
    c = q.shape[2]
    G = jnp.cumsum(g, axis=-1)
    diff = G[..., :, None] - G[..., None, :]
    lower = jnp.tril(jnp.ones((c, c), dtype=bool))
    strict = jnp.tril(jnp.ones((c, c), dtype=bool), -1)
    decay = jnp.exp(jnp.where(lower, diff, -jnp.inf))
    kb = k * beta[..., None]
    A = jnp.einsum('bhid,bhjd->bhij', kb, k) * jnp.where(strict, decay, 0.0)
    eye = jnp.eye(c, dtype=jnp.float32)
    rhs = jnp.concatenate([v * beta[..., None], kb * jnp.exp(G)[..., None]], axis=-1)
    sol = lax.linalg.triangular_solve(A + eye, rhs, left_side=True, lower=True, unit_diagonal=True)
    u, w = sol[..., :GDN_DV], sol[..., GDN_DV:]
    v_new = u - jnp.einsum('bhik,bhkv->bhiv', w, S)
    attn = jnp.einsum('bhik,bhjk->bhij', q, k) * decay
    o = jnp.einsum('bhik,bhkv->bhiv', q * jnp.exp(G)[..., None], S) + jnp.einsum('bhij,bhjv->bhiv', attn, v_new)
    G_last = G[..., -1:]
    S_new = S * jnp.exp(G_last)[..., None] + jnp.einsum('bhik,bhiv->bhkv', k * jnp.exp(G_last - G)[..., None], v_new)
    return S_new, o

def token_mixer(h, pos, s_ret, s_gdn, s_conv, w_in, conv_w, a_log, dt_bias, gdn_norm_w,
                w_branch_a, w_branch_b, w_out):
    B, L, _ = h.shape
    dt = h.dtype
    f32 = jnp.float32
    p = h @ w_in
    split_idx = np.cumsum(IN_SPLITS)[:-1].tolist()
    q_r, k_r, v_r, g_r, qkv_g, z_g, a_g, b_g, gate_a, gate_b = jnp.split(p, split_idx, axis=-1)
    tr = lambda a: jnp.swapaxes(a, 1, 2)

    lg = jnp.log1p(-jnp.exp2(-5.0 - jnp.arange(RET_HEADS, dtype=f32)))
    q = rotary(q_r.reshape(B, L, RET_HEADS, RET_DK).astype(f32), pos)
    k = rotary(k_r.reshape(B, L, RET_HEADS, RET_DK).astype(f32), pos) * (RET_DK ** -0.5)
    v = v_r.reshape(B, L, RET_HEADS, RET_DV).astype(f32)
    s_ret_new, o = chunk_scan(functools.partial(retention_step, lg), s_ret.astype(f32),
                              (tr(q), tr(k), tr(v)), RET_CHUNK)
    o = rms_normalize(tr(o)).reshape(B, L, RET_V_W)
    o_ret = (o * jax.nn.silu(g_r.astype(f32))).astype(dt)

    xc = jnp.concatenate([s_conv.astype(dt), qkv_g], axis=1)
    acc = xc[:, 0:L].astype(f32) * conv_w[0].astype(f32)
    for i in range(1, CONV_W):
        acc = acc + xc[:, i:i + L].astype(f32) * conv_w[i].astype(f32)
    s_conv_new = xc[:, L:]
    u = jax.nn.silu(acc)
    qg, kg, vg = jnp.split(u, [GDN_QK_W, 2 * GDN_QK_W], axis=-1)
    qg = l2norm(qg.reshape(B, L, GDN_HEADS, GDN_DK)) * (GDN_DK ** -0.5)
    kg = l2norm(kg.reshape(B, L, GDN_HEADS, GDN_DK))
    vg = vg.reshape(B, L, GDN_HEADS, GDN_DV)
    g = -jnp.exp(a_log.astype(f32)) * jax.nn.softplus(a_g.astype(f32) + dt_bias.astype(f32))
    beta = jax.nn.sigmoid(b_g.astype(f32))
    s_gdn_new, og = chunk_scan(gdn_step, s_gdn.astype(f32),
                               (tr(qg), tr(kg), tr(vg), tr(g), tr(beta)), GDN_CHUNK)
    og = rms_normalize(tr(og)) * gdn_norm_w.astype(f32)
    og = og * jax.nn.silu(z_g.astype(f32).reshape(B, L, GDN_HEADS, GDN_DV))
    o_gdn = og.reshape(B, L, GDN_V_W).astype(dt)

    ya = o_ret @ w_branch_a
    yb = o_gdn @ w_branch_b
    m = jax.nn.sigmoid(gate_a) * ya + jax.nn.sigmoid(gate_b) * yb
    return m @ w_out, s_ret_new, s_gdn_new, s_conv_new

def moe_ffn(h, w_router, b_router, w_gate_up, b_gate_up, w_down, b_down):
    B, L, D = h.shape
    T = B * L
    f32 = jnp.float32
    x2 = h.reshape(T, D)
    logits = x2.astype(f32) @ w_router.astype(f32) + b_router.astype(f32)
    top_v, top_i = lax.top_k(logits, TOP_K)
    gate = jax.nn.softmax(top_v, axis=-1)
    n = T * TOP_K
    flat_e = top_i.reshape(n).astype(jnp.int32)
    flat_w = gate.reshape(n)
    flat_t = jnp.arange(n, dtype=jnp.int32) // TOP_K
    order = jnp.argsort(flat_e)
    se = flat_e[order]
    counts = jnp.bincount(flat_e, length=N_EXPERTS)
    start = jnp.cumsum(counts) - counts
    pcounts = (counts + MOE_BLOCK - 1) // MOE_BLOCK * MOE_BLOCK
    pend = jnp.cumsum(pcounts)
    pstart = pend - pcounts
    dest = pstart[se] + (jnp.arange(n, dtype=jnp.int32) - start[se])
    R = (-(-n // MOE_BLOCK) + N_EXPERTS) * MOE_BLOCK
    nb = R // MOE_BLOCK
    rows_t = jnp.full((R,), T, dtype=jnp.int32).at[dest].set(flat_t[order])
    rows_w = jnp.zeros((R,), f32).at[dest].set(flat_w[order])
    block_e = jnp.minimum(jnp.searchsorted(pend, jnp.arange(nb, dtype=jnp.int32) * MOE_BLOCK, side='right'),
                          N_EXPERTS - 1)
    xs = jnp.concatenate([x2, jnp.zeros((1, D), x2.dtype)], axis=0)[rows_t].reshape(nb, MOE_BLOCK, D)

    def expert_block(args):
        xb, e = args
        hb = (xb @ w_gate_up[e] + b_gate_up[e]).astype(f32)
        glu = jnp.minimum(hb[:, :D_FF], SWIGLU_LIMIT)
        lin = jnp.clip(hb[:, D_FF:], -SWIGLU_LIMIT, SWIGLU_LIMIT)
        act = (glu * jax.nn.sigmoid(SWIGLU_ALPHA * glu) * (lin + 1.0)).astype(xb.dtype)
        return act @ w_down[e] + b_down[e]

    ys = lax.map(expert_block, (xs, block_e))
    out = jnp.zeros((T + 1, D), f32).at[rows_t].add(ys.reshape(R, D).astype(f32) * rows_w[:, None])
    return out[:T].reshape(B, L, D).astype(h.dtype)

def decoder_layer(x, pos, s_ret, s_gdn, s_conv, attn_norm_w, w_in, conv_w, a_log, dt_bias, gdn_norm_w,
                  w_branch_a, w_branch_b, w_out, ffn_norm_w, w_router, b_router, w_gate_up, b_gate_up,
                  w_down, b_down):
    mix, sr, sg, sc = token_mixer(rmsnorm(x, attn_norm_w), pos, s_ret, s_gdn, s_conv, w_in, conv_w, a_log,
                                  dt_bias, gdn_norm_w, w_branch_a, w_branch_b, w_out)
    x = x + mix
    x = x + moe_ffn(rmsnorm(x, ffn_norm_w), w_router, b_router, w_gate_up, b_gate_up, w_down, b_down)
    return x, sr, sg, sc

def setup_inputs(seed: int = 0) -> dict:
    key = jax.random.key(seed)
    ks = jax.random.split(key, 24)
    f32 = jnp.float32

    def nrm(k, shape, scale):
        return jax.random.normal(k, shape, f32) * scale

    x_prompt = nrm(ks[0], (BATCH, SEQ, D_MODEL), 1.0)
    x_sample = nrm(ks[1], (DEC_BATCH, DEC_SEQ, D_MODEL), 1.0)
    state_ret = nrm(ks[2], (DEPTH, DEC_BATCH, RET_HEADS, RET_DK, RET_DV), RET_DK ** -0.5)
    state_gdn = nrm(ks[3], (DEPTH, DEC_BATCH, GDN_HEADS, GDN_DK, GDN_DV), GDN_DK ** -0.5)
    state_conv = nrm(ks[4], (DEPTH, DEC_BATCH, CONV_W - 1, CONV_CH), 1.0)
    attn_norm_w = 1.0 + nrm(ks[5], (DEPTH, D_MODEL), 0.02)
    w_in = nrm(ks[6], (DEPTH, D_MODEL, IN_WIDTH), D_MODEL ** -0.5)
    conv_w = nrm(ks[7], (DEPTH, CONV_W, CONV_CH), CONV_W ** -0.5)
    a_log = jnp.log(jax.random.uniform(ks[8], (DEPTH, GDN_HEADS), f32, 1.0, 16.0))
    dtv = jnp.exp(jax.random.uniform(ks[9], (DEPTH, GDN_HEADS), f32, math.log(1e-3), math.log(1e-1)))
    dt_bias = dtv + jnp.log(-jnp.expm1(-dtv))
    gdn_norm_w = 1.0 + nrm(ks[10], (DEPTH, GDN_DV), 0.02)
    w_branch_a = nrm(ks[11], (DEPTH, RET_V_W, D_MODEL), RET_V_W ** -0.5)
    w_branch_b = nrm(ks[12], (DEPTH, GDN_V_W, D_MODEL), GDN_V_W ** -0.5)
    w_out = nrm(ks[13], (DEPTH, D_MODEL, D_MODEL), D_MODEL ** -0.5)
    ffn_norm_w = 1.0 + nrm(ks[14], (DEPTH, D_MODEL), 0.02)
    w_router = nrm(ks[15], (DEPTH, D_MODEL, N_EXPERTS), D_MODEL ** -0.5)
    b_router = nrm(ks[16], (DEPTH, N_EXPERTS), 0.01)
    w_gate_up = nrm(ks[17], (DEPTH, N_EXPERTS, D_MODEL, 2 * D_FF), D_MODEL ** -0.5)
    b_gate_up = nrm(ks[18], (DEPTH, N_EXPERTS, 2 * D_FF), 0.01)
    w_down = nrm(ks[19], (DEPTH, N_EXPERTS, D_FF, D_MODEL), D_FF ** -0.5)
    b_down = nrm(ks[20], (DEPTH, N_EXPERTS, D_MODEL), 0.01)
    final_norm_w = 1.0 + nrm(ks[21], (D_MODEL,), 0.02)
    return {"x_prompt": x_prompt, "x_sample": x_sample, "state_ret": state_ret, "state_gdn": state_gdn,
            "state_conv": state_conv, "attn_norm_w": attn_norm_w, "w_in": w_in, "conv_w": conv_w,
            "a_log": a_log, "dt_bias": dt_bias, "gdn_norm_w": gdn_norm_w, "w_branch_a": w_branch_a,
            "w_branch_b": w_branch_b, "w_out": w_out, "ffn_norm_w": ffn_norm_w, "w_router": w_router,
            "b_router": b_router, "w_gate_up": w_gate_up, "b_gate_up": b_gate_up, "w_down": w_down,
            "b_down": b_down, "final_norm_w": final_norm_w}

def reference(x_prompt, x_sample, state_ret, state_gdn, state_conv, attn_norm_w, w_in, conv_w, a_log, dt_bias,
              gdn_norm_w, w_branch_a, w_branch_b, w_out, ffn_norm_w, w_router, b_router, w_gate_up, b_gate_up,
              w_down, b_down, final_norm_w):
    f32 = jnp.float32
    Bp, Lp = x_prompt.shape[0], x_prompt.shape[1]
    pos_p = jnp.arange(Lp, dtype=jnp.int32)
    pos_s = PAST_LEN + jnp.arange(x_sample.shape[1], dtype=jnp.int32)
    z_ret = jnp.zeros((Bp, RET_HEADS, RET_DK, RET_DV), f32)
    z_gdn = jnp.zeros((Bp, GDN_HEADS, GDN_DK, GDN_DV), f32)
    z_conv = jnp.zeros((Bp, CONV_W - 1, CONV_CH), x_prompt.dtype)
    xp, xs = x_prompt, x_sample
    rp, gp, cp, rs, gs, cs = [], [], [], [], [], []
    for l in range(DEPTH):
        lw = (attn_norm_w[l], w_in[l], conv_w[l], a_log[l], dt_bias[l], gdn_norm_w[l], w_branch_a[l],
              w_branch_b[l], w_out[l], ffn_norm_w[l], w_router[l], b_router[l], w_gate_up[l], b_gate_up[l],
              w_down[l], b_down[l])
        xp, a1, a2, a3 = decoder_layer(xp, pos_p, z_ret, z_gdn, z_conv, *lw)
        xs, b1, b2, b3 = decoder_layer(xs, pos_s, state_ret[l], state_gdn[l], state_conv[l], *lw)
        rp.append(a1); gp.append(a2); cp.append(a3)
        rs.append(b1); gs.append(b2); cs.append(b3)
    y_prompt = rmsnorm(xp, final_norm_w)
    y_sample = rmsnorm(xs, final_norm_w)
    ret_prompt = jnp.stack(rp).astype(state_ret.dtype)
    gdn_prompt = jnp.stack(gp).astype(state_gdn.dtype)
    conv_prompt = jnp.stack(cp).astype(state_conv.dtype)
    ret_sample = jnp.stack(rs).astype(state_ret.dtype)
    gdn_sample = jnp.stack(gs).astype(state_gdn.dtype)
    conv_sample = jnp.stack(cs).astype(state_conv.dtype)
    return (y_prompt, y_sample, ret_prompt, gdn_prompt, conv_prompt, ret_sample, gdn_sample, conv_sample)


_drawn_inputs = setup_inputs


def setup_inputs(seed=0):
    import zlib

    import numpy as np

    out = dict(_drawn_inputs(seed))
    spreads = {}
    factors = {'b_gate_up': 8.0, 'b_down': 8.0, 'final_norm_w': 2.749}
    for name, (base, spread) in spreads.items():
        noise = np.random.default_rng([zlib.crc32(name.encode()), seed]).standard_normal(out[name].shape)
        drawn = base * np.exp(spread * noise) if base else spread * noise
        out[name] = __import__('jax').numpy.asarray(drawn.astype(out[name].dtype))
    for name, factor in factors.items():
        out[name] = (out[name] * factor).astype(out[name].dtype)
    return out
```

```python
from contextlib import ExitStack

import numpy as np
import concourse.bass as bass
from concourse import mybir

ALU = mybir.AluOpType
ACT = mybir.ActivationFunctionType
F32 = mybir.dt.float32
U32 = mybir.dt.uint32
I32 = mybir.dt.int32
AX = mybir.AxisListType

P = 128
D = 1024
KT = D // P
NB, PAST = 8, 2048
TOK = 256 + NB
TILES = [(0, P), (1, P), (2, NB)]
RH, RDV = 4, 256
GH = 8
CCH = 3 * GH
EPS = 1e-6
IN_W = 9232
Z0, GA0, GB0 = 3072, 4096, 5120
PW = 6144
AB = 7168
NE, TOPK, SLOTS = 32, 4, 64
NM = -(-TOK // SLOTS)
NEXTRA = (TOK * TOPK - NE) // SLOTS
DUMP = 2 * TOK
ROWS = DUMP + P
LOGG = [float(np.log1p(-np.exp2(np.float32(-5.0 - h)))) for h in range(RH)]

C_ID, C_INC, C_ONE, C_LVL = 0, P, 2 * P, 3 * P
C_DM = C_LVL + 7 * P
C_TRIG = C_DM + RH * P
C_QD = C_TRIG + 3 * 2 * 2 * 64
C_KD = C_QD + RH
C_TID = C_KD + RH
C_SLOT = C_TID + 3
C_DIX = C_SLOT + P
C_J = C_DIX + 2
C_QV = C_J + NEXTRA
C_DIAG = C_QV + NE * (NM - 1)
C_NC = C_DIAG + NB * NB


def constants():
    t = np.zeros((P, C_NC), np.float64)
    i = np.arange(P)
    row, col = i[:, None], i[None, :]
    t[:, C_ID:C_ID + P] = row == col
    t[:, C_INC:C_INC + P] = row <= col
    t[:, C_ONE:C_ONE + P] = 1.0
    for lv in range(7):
        s = 1 << lv
        t[:, C_LVL + lv * P:C_LVL + (lv + 1) * P] = (
            (row // (2 * s) == col // (2 * s)) & (row % (2 * s) < s) & (col % (2 * s) >= s))
    for h in range(RH):
        t[:, C_DM + h * P:C_DM + (h + 1) * P] = np.where(row <= col, np.exp((col - row) * LOGG[h]), 0.0)
        t[:, C_QD + h] = np.exp((i + 1) * LOGG[h])
        t[:, C_KD + h] = np.exp((P - 1 - i) * LOGG[h])
    inv = (1.0 / (np.float32(10000.0) ** (np.arange(64, dtype=np.float32) / np.float32(64)))).astype(np.float32)
    for c, _ in TILES:
        pos = (i + P * c if c < 2 else np.full(P, PAST)).astype(np.float32)
        ang = (pos[:, None] * inv[None, :]).astype(np.float32).astype(np.float64)
        for cs, f in enumerate((np.cos, np.sin)):
            for qk, sc in enumerate((1.0, P ** -0.5)):
                o = C_TRIG + ((c * 2 + cs) * 2 + qk) * 64
                t[:, o:o + 64] = f(ang) * sc
    for c, _ in TILES:
        t[:, C_TID + c] = P * c + i + 1
    t[:, C_SLOT:C_SLOT + P] = col % SLOTS
    t[:, C_DIX] = (i // SLOTS) - 2 - DUMP - i
    t[:, C_DIX + 1] = DUMP + i
    t[:, C_J:C_J + NEXTRA] = np.arange(NEXTRA) + 1
    t[:, C_QV:C_QV + NE * (NM - 1)] = np.arange(NE, NE * NM)
    t[:, C_DIAG:C_NC] = np.eye(NB).reshape(-1)
    return t.astype(np.float32)


def build_layer(nc, d, o):
    with ExitStack() as ctx:
        base = [-(-nc.sbuf_base // 32) * 32]

        def at(name, offset, shape, dt=F32):
            return nc.alloc_sbuf_tensor_at(name, shape, dt, offset=offset)

        def new(name, shape, dt=F32):
            n = 4
            for s in shape[1:]:
                n *= s
            t = at(name, base[0], shape, dt)
            base[0] += -(-n // 32) * 32
            return t

        def sem(name):
            return ctx.enter_context(nc.semaphore(name))

        def bank(i):
            return ctx.enter_context(nc.psum_tensor(f"bank{i}", [P, 512], F32))

        wreg = base[0]
        base[0] += 96 * 1024
        wslot = [at(f"wslot{u}", wreg + 16384 * u, [P, KT, 512]) for u in range(2)]
        scr = wreg + 32768
        htok = at("htok", scr, [P, 3, D])
        ut0 = wreg + 65536
        uT = at("uT", ut0, [P, CCH, TOK])
        raw = at("raw", ut0 + 25600, [P, 2, 259])
        p0 = base[0]
        Pt = new("Pt", [P, 2, PW])
        ps0 = base[0]
        Ps = new("Ps", [P, PW])
        X = new("X", [P, 3, D])
        ht0 = base[0]
        HT = new("HT", [P, KT, TOK])
        K = new("K", [P, C_NC])
        WN = new("WN", [P, D])
        edges = new("edges", [P, CCH, 11])
        cw = new("cw", [P, CCH, 4])
        wab = new("wab", [P, KT, 2 * GH])
        cwr = new("cwr", [4 * CCH, P])
        ss = new("ss", [P, 3])
        rs = new("rs", [P, 3])
        eps = new("eps", [P, 1])
        gts = new("gts", [P, 3, 2 * GH])
        gl = new("gl", [P, 3, GH])
        beta = new("beta", [P, 3, GH])
        gt1 = new("gt1", [P, 3, GH])
        gt2 = new("gt2", [P, 3, GH])
        prm = new("prm", [P, 2, GH])
        Gc = new("Gc", [P, GH])
        eG = new("eG", [P, GH])
        kds = new("kds", [P, GH])
        eGl = new("eGl", [P, GH])
        beG = new("beG", [P, GH])
        rr = new("rr", [P, 3, GH])
        assert base[0] <= nc.sbuf_usable_end, base[0]
        hist = at("hist", scr + 12288, [24, 3 * D])
        histT = at("histT", ut0 + 25600 + 2080, [P, CCH, 24])
        ctok = at("ctok", scr, [11, 3 * D])
        sq = at("sq", scr + 12288, [P, 2 * GH, TOK])
        qkr = at("qkr", scr, [P, 2, D])
        qkrs = at("qkrs", scr + 8192, [P, D])
        rt = at("rt", scr + 12288, [P, 4, RH, 64])
        kdr = at("kdr", scr + 16384, [P, 2, RH, P])
        inT = at("inT", scr + 20480, [P, 2, RH, P])
        Sr = at("Sr", scr + 24576, [P, RH, RDV])
        sqr = at("sqr", scr + 28672, [P, D])
        sqr_s = at("sqr_s", p0 + 4 * PW + 4096, [P, D])
        Ssr = [at(f"Ssr{u}", scr + 12288 + 8192 * u, [P, NB, RDV]) for u in range(2)]
        kms = at("kms", scr, [NB, NB, P])
        qmr = at("qmr", scr + 4096, [P, RH, NB, NB])
        At, U, T, Y, Al0, Al1, attnT, kdg = [at(n, scr + 4096 * i, [P, GH, P]) for i, n in enumerate(
            ["At", "U", "T", "Y", "Al0", "Al1", "attnT", "kdg"])]
        bv, kbG = [at(n, p0 + 4096 * i, [P, GH, P]) for i, n in enumerate(["bv", "kbG"])]
        vn, wTn = [at(n, p0 + 4 * PW + 4096 * i, [P, GH, P]) for i, n in enumerate(["vn", "wTn"])]
        Sg, tmpF = [at(n, ps0 + 4096 * i, [P, GH, P]) for i, n in enumerate(["Sg", "tmpF"])]
        DT, gB = [at(n, ht0 + 4096 * i, [P, GH, P]) for i, n in enumerate(["DT", "gB"])]
        gnw = at("gnw", ut0 + 25600 + 2080 + 2304, [P, P])
        Ssg = at("Ssg", scr, [P, NB, GH, P])
        ksm = at("ksm", p0, [NB, D])
        vsm = at("vsm", p0 + 4096, [NB, D])
        vm = [at(f"vm{u}", p0 + 4 * PW + 4096 * u, [NB, NB, P]) for u in range(2)]
        qmg, kmg = [at(n, ut0 + 25600 + 2080 * i, [P, GH, NB, NB]) for i, n in enumerate(["qmg", "kmg"])]
        egd = at("egd", ut0 + 30496, [NB, GH, NB])
        egb = at("egb", ut0 + 30752, [P, 64])
        osg = at("osg", ps0 + 4096, [P, D])
        OTb = at("OTb", ut0, [P, KT, TOK])
        mb = [p0]

        def mnew(name, shape, dt=F32):
            n = 4
            for x in shape[1:]:
                n *= x
            t = at(name, mb[0], shape, dt)
            mb[0] += -(-n // 32) * 32
            assert mb[0] <= ps0 + 4 * PW
            return t
        wr = mnew("wr", [P, KT, NE])
        br = mnew("br", [1, NE])
        Lg, gt, eq, sel, ex = [mnew(n, [P, 3, NE]) for n in ("Lg", "gt", "eq", "sel", "ex")]
        mx = mnew("mx", [P, 3, 8])
        red = mnew("red", [P, 3])
        Z = mnew("Z", [P, 3, NE])
        R0 = mnew("R0", [P, 3, NE])
        R = mnew("R", [P, 3, NM * NE])
        cnt = mnew("cnt", [1, NE])
        NX = NE * (NM - 1)
        xval, xpre, xev = [mnew(n, [1, NX]) for n in ("xval", "xpre", "xev")]
        xcmp, xtmp = [mnew(n, [1, NEXTRA, NX]) for n in ("xcmp", "xtmp")]
        xql, xel = mnew("xql", [1, NEXTRA]), mnew("xel", [1, NEXTRA])
        xqi, xei, xni = mnew("xqi", [1, NEXTRA], I32), mnew("xei", [1, NEXTRA], I32), mnew("xni", [1, 1], I32)
        zrow = mnew("zrow", [P, 512])
        O = mnew("O", [P, 3, P])
        tw = mnew("tw", [P, 3, 2])
        vt = mnew("vt", [P, NE + NEXTRA, 2])
        ia, ib = mnew("ia", [P, 1]), mnew("ib", [P, 1])
        sa, sb_ = mnew("sa", [P, 1]), mnew("sb_", [P, 1])
        gidx, sidx = mnew("gidx", [P, 1], U32), mnew("sidx", [P, 1], U32)
        xg, glu, lin, sg, ac, yb = [mnew(n, [P, 512]) for n in ("xg", "glu", "lin", "sg", "ac", "yb")]
        xT, acT = mnew("xT", [P, 4, P]), mnew("acT", [P, 4, P])
        bgu, bdn = mnew("bgu", [1, 2 * D]), mnew("bdn", [1, D])
        gus = [at(f"gus{k}", wreg + 8192 * k, [P, 2 * D]) for k in range(KT)]
        dns = [at(f"dns{k}", wreg + 65536 + 8192 * k, [P, 2, D]) for k in range(KT // 2)]
        x2d = nc.dram_tensor("x2d", [ROWS, 512], F32, kind="Internal").ap()
        acc_d = nc.dram_tensor("acc_d", [ROWS, 512], F32, kind="Internal").ap()
        B = [bank(i) for i in range(8)]

        def Prow(c):
            return Pt[:, c, :] if c < 2 else Ps[0:NB, :]

        ident = K[:, C_ID:C_ID + P]
        ones = K[:, C_ONE:C_ONE + P]
        diag = K[:, C_DIAG:C_NC].rearrange("p (b m) -> p b m", b=NB)

        def quad(b, n=P):
            return b[:, 0:4 * n].rearrange("p (j n) -> p j n", j=4)

        def bc(ap, n, axis=2):
            a = ap.unsqueeze(axis)
            shape = list(a.shape)
            shape[axis] = n
            return a.broadcast_to(shape)

        def half(f, i):
            return f[:, 4 * i:4 * i + 4, :]

        inc = K[:, C_INC:C_INC + P]

        class Order:

            def __init__(self, s, names):
                self.s, self.names, self.n = s, names, 0
                assert len(set(names)) == len(names)

            def value(self, name):
                return self.names.index(name) + 1

            def did(self, ins, name):
                assert self.names[self.n] == name, (self.names[self.n], name)
                self.n += 1
                ins.then_inc(self.s, 1)

            def wait(self, eng, name):
                eng.wait_ge(self.s, self.value(name))

        s_const, s_wn, s_tables = sem("s_const"), sem("s_wn"), sem("s_tables")
        s_x = [sem(f"s_x{c}") for c in range(3)]
        s_back = [sem(f"s_back{c}") for c in range(3)]
        s_wab, s_cwr, s_ab, s_cwT, s_abev, s_cw = [sem(n) for n in ("s_wab", "s_cwr", "s_ab", "s_cwT", "s_abev", "s_cw")]
        s_w = [sem(f"s_w{u}") for u in range(2)]
        s_ss, s_h, s_tr, s_trev = sem("s_ss"), sem("s_h"), sem("s_tr"), sem("s_trev")
        s_ct, s_raw, s_cvc, s_cv = sem("s_ct"), sem("s_raw"), sem("s_cvc"), sem("s_cv")
        s_pt, s_pfA, s_pfD = sem("s_pt"), sem("s_pfA"), sem("s_pfD")
        s_init, s_out, s_rs = sem("s_init"), sem("s_out"), sem("s_rs")
        dve_chain, act_chain, pool_chain = sem("dve_chain"), sem("act_chain"), sem("pool_chain")

        s_hist, s_hT, s_hTev, s_eT, s_eTev = sem("s_hist"), sem("s_hT"), sem("s_hTev"), sem("s_eT"), sem("s_eTev")
        s_sconv, s_silu, s_sq = sem("s_sconv"), sem("s_silu"), sem("s_sq")
        s_l2, s_l2r, s_l2d = sem("s_l2"), sem("s_l2r"), sem("s_l2d")
        s_rot, s_in, s_inT, s_kdr, s_rm, s_Sr, s_ro = [sem(n) for n in (
            "s_rot", "s_in", "s_inT", "s_kdr", "s_rm", "s_Sr", "s_ro")]
        s_sr = [sem(f"s_sr{u}") for u in range(2)]
        s_km, s_qm, s_out1, s_sup, s_oc, s_osd = [sem(n) for n in (
            "s_km", "s_qm", "s_out1", "s_sup", "s_oc", "s_osd")]
        s_sg, s_hss, s_hrt, s_on = [sem(n) for n in ("s_sg", "s_hss", "s_hrt", "s_on")]
        s_prm, s_gv, s_ga = sem("s_prm"), sem("s_gv"), sem("s_ga")
        s_retout, s_gdnout, s_gsout, s_sgl = sem("s_retout"), sem("s_gdnout"), sem("s_gsout"), sem("s_sgl")

        def mm_names(c):
            n = [f"G.{c}"]
            for x in ["Gbc", "Bbc", "KK", "kT", "QK", "vT", "T1"]:
                n += [f"{x}{i}.{c}" for i in range(2)]
            for lv in range(1, 7):
                for x in (["Y", "dT", "dU"] if lv < 6 else ["Y", "dU"]):
                    n += [f"{x}{lv}.{i}.{c}" for i in range(2)]
            for x in (["wT"] if c else []) + ["u", "o"] + (["qS"] if c else []) + ["dS"]:
                n += [f"{x}{i}.{c}" for i in range(2)]
            return n

        def dve_names(c):
            n = [f"Gc.{c}", f"D0.{c}", f"D1.{c}", f"kd.{c}", f"min.{c}", f"mask.{c}"]
            n += [f"dB0.{c}", f"dB1.{c}", f"At0.{c}", f"At1.{c}", f"kdg0.{c}", f"kdg1.{c}"]
            n += ([f"beG.{c}", f"kbG0.{c}", f"kbG1.{c}"] if c else [])
            n += [f"U0.{c}", f"U1.{c}", f"attn0.{c}", f"attn1.{c}", f"bv0.{c}", f"bv1.{c}"]
            for lv in range(1, 7):
                for x in (["T", "U"] if lv < 6 else ["U"]):
                    n += [f"{x}{lv}.{i}.{c}" for i in range(2)]
            n += [f"O0.{c}", f"O1.{c}"] + ([f"Oa0.{c}", f"Oa1.{c}"] if c else []) + [f"S0.{c}", f"S1.{c}"]
            return n

        def act_names(c):
            n = [f"eG.{c}", f"eGl.{c}", f"kds.{c}", f"exp.{c}", f"T0.{c}", f"T1.{c}"]
            for lv in range(1, 7):
                n += [f"Y{lv}.{i}.{c}" for i in range(2)]
            n += ([f"wT0.{c}", f"wT1.{c}"] if c else []) + [f"vn0.{c}", f"vn1.{c}"]
            return n

        def pool_names(c):
            return [f"gB.{c}", f"bB.{c}"] + [f"Al{lv}.{c}" for lv in range(7)]

        def chunk_of(i, c):
            return uT[:, GH * i:GH * i + GH, P * c:P * c + P]

        MM = Order(sem("gdn_products"), mm_names(0) + mm_names(1))
        DV = Order(sem("gdn_dve"), dve_names(0) + dve_names(1))
        AC = Order(sem("gdn_act"), act_names(0) + act_names(1))
        PL = Order(sem("gdn_pool"), pool_names(0) + pool_names(1))
        MS = Order(sem("gds_products"), ["egb", "k", "v", "kS", "out0"]
                   + [x for h in range(1, GH) for x in (f"out{h}", f"oc{h - 1}")] + [f"oc{GH - 1}"])
        DS = Order(sem("gds_dve"), ["eg", "egd", "ksm", "vsm", "vn1", "vn2", "vn3"]
                   + [f"S{h}" for h in range(GH)] + ["osg"])
        AS = Order(sem("gds_act"), ["eg", "egb"])
        PS = Order(sem("gds_pool"), ["qmg", "kmg"] + [f"vm{h}" for h in range(GH)])

        s_bw = [sem(f"s_bw{u}") for u in range(2)]
        s_sig, s_bt, s_bd, s_bev, s_wr = sem("s_sig"), sem("s_bt"), sem("s_bd"), sem("s_bev"), sem("s_wr")
        s_mix, s_res = sem("s_mix"), sem("s_res")
        s_xd, s_zd, s_zr, s_lg, s_ex, s_exd, s_sel, s_pos, s_tab, s_ext = [sem(n) for n in (
            "s_xd", "s_zd", "s_zr", "s_lg", "s_ex", "s_exd", "s_sel", "s_pos", "s_tab", "s_ext")]
        m_wgu = [sem(f"m_wgu{k}") for k in range(KT)]
        m_wd = [sem(f"m_wd{k}") for k in range(KT // 2)]
        (m_bgu, m_bdn, m_im, m_tx, m_guc, m_gu, m_ta, m_dc, m_d, m_taev, m_txev, m_sig, m_yev, m_O, m_v, m_gi, m_gic,
         m_si, m_sic, m_glu, m_lin, m_gl, m_act, m_g, m_s) = [sem(n) for n in (
             "m_bgu", "m_bdn", "m_im", "m_tx", "m_guc", "m_gu", "m_ta", "m_dc", "m_d", "m_taev", "m_txev", "m_sig",
             "m_yev", "m_O", "m_v", "m_gi", "m_gic", "m_si", "m_sic", "m_glu", "m_lin", "m_gl", "m_act", "m_g", "m_s")]
        m_go, s_moe, s_fin = sem("m_go"), sem("s_moe"), sem("s_fin")

        def after(eng, s, per, b, plus=0):
            if isinstance(b, int) and b * per + plus <= 0:
                return
            eng.wait_ge(s, b * per + plus)

        def extra_blocks(eng, body):
            eng.wait_ge(s_ext, 2)
            many = eng.value_load(xni[0:1, 0:1], min_val=0, max_val=NEXTRA)
            with eng.If(many > 0):
                with eng.Fori(0, NEXTRA) as j:
                    with eng.If(j < many):
                        body(j, j + NE)

        def chain(eng, s):
            n = [0]

            def link(ins):
                n[0] += 1
                ins.then_inc(s, 1)
                eng.wait_ge(s, n[0])
            return link

        block = ctx.enter_context(nc.Block())
        w_in = d["w_in"][0].rearrange("(k p) n -> p k n", p=P)

        @block.sync
        def _(sp):
            for c in range(2):
                sp.dma_start(X[:, c, :], d["x_prompt"][0][P * c:P * c + P, :]).then_inc(s_x[c], 16)
            sp.dma_start(X[0:NB, 2, :], d["x_sample"].rearrange("b l n -> (b l) n")).then_inc(s_x[2], 16)
            sp.dma_start(WN[:, :], d["attn_norm_w"].broadcast_to([P, D])).then_inc(s_wn, 16)
            sp.dma_start(K[:, 0:C_LVL], d["consts"][:, 0:C_LVL]).then_inc(s_const, 16)
            sp.dma_start(cwr[:, :], d["conv_w"][0].rearrange("i (c p) -> (i c) p", p=P)).then_inc(s_cwr, 16)
            sp.dma_start(wab[:, :, :], w_in[:, :, AB:AB + 2 * GH]).then_inc(s_wab, 16)
            sp.dma_start(wslot[0][:, :, :], w_in[:, :, 3072:3584]).then_inc(s_w[0], 16)
            sp.dma_start(prm[:, 0, :], d["a_log"].broadcast_to([P, GH])).then_inc(s_prm, 16)
            sp.dma_start(prm[:, 1, :], d["dt_bias"].broadcast_to([P, GH])).then_inc(s_prm, 16)
            sp.dma_start(gnw[:, :], d["gdn_norm_w"].broadcast_to([P, P])).then_inc(s_prm, 16)
            sp.dma_start(wslot[1][:, :, :], w_in[:, :, 3584:4096]).then_inc(s_w[1], 16)
            sp.dma_start(K[:, C_LVL:C_NC], d["consts"][:, C_LVL:C_NC]).then_inc(s_tables, 16)
            sp.dma_start(hist[:, :], d["state_conv"][0].rearrange("b i n -> (b i) n")).then_inc(s_hist, 16)
            with sp.Fori(1, 3) as i:
                for u in range(2):
                    sp.wait_ge(s_ct, i * 8 + 4 * u - 4)
                    sp.dma_start(wslot[u][:, :, :],
                                 w_in[:, :, bass.ds(i * 1024 + 3072 + 512 * u, 512)]).then_inc(s_w[u], 16)
            for u in range(2):
                sp.wait_ge(s_ct, 20 + 4 * u)
                sp.dma_start(wslot[u][:, :, :], w_in[:, :, 512 * u:512 * u + 512]).then_inc(s_w[u], 16)
            for first, last, col in ((1, 3, 0), (3, 4, 3072), (4, 6, 3072 + 2 * GH)):
                with sp.Fori(first, last) as i:
                    for u in range(2):
                        sp.wait_ge(s_pt, i * 6 + 3 * u - 3)
                        sp.dma_start(wslot[u][:, :, :],
                                     w_in[:, :, bass.ds(i * 1024 + col + 512 * u, 512)]).then_inc(s_w[u], 16)

            wb = [d[n][0].rearrange("(k p) n -> p k n", p=P) for n in ("w_branch_a", "w_branch_b", "w_out")]

            def load_branch(r):
                sp.dma_start(wslot[r % 2][:, :, :], wb[r // 2][:, :, 512 * (r % 2):512 * (r % 2) + 512]
                             ).then_inc(s_bw[r % 2], 16)
            sp.wait_ge(s_h, 3)
            sp.dma_start(WN[:, :], d["ffn_norm_w"].broadcast_to([P, D])).then_inc(s_wn, 16)
            sp.wait_ge(s_pt, 33)
            load_branch(0)
            sp.wait_ge(s_pt, 36)
            load_branch(1)
            sp.wait_ge(s_Sr, 2)
            sp.dma_start(o[2][0, 0].rearrange("h k v -> k h v"), Sr[:, :, :]).then_inc(s_retout, 16)
            for h in range(RH):
                if h == 0:
                    sp.wait_ge(s_retout, 16)
                    sp.wait_ge(s_ro, 3)
                if h >= 2:
                    sp.wait_ge(s_retout, 16 * (h - 1) + 16)
                    sp.wait_ge(s_oc, h - 1)
                sp.dma_start(Ssr[h % 2][:, :, :], d["state_ret"][0, :, h].rearrange("b k v -> k b v")).then_inc(s_sr[h % 2], 16)
                if h >= 1:
                    sp.wait_ge(s_sup, h)
                    sp.dma_start(o[5][0, :, h - 1].rearrange("b k v -> k b v"), Ssr[(h - 1) % 2][:, :, :]
                                 ).then_inc(s_retout, 16)
            sp.wait_ge(s_sup, RH)
            sp.dma_start(o[5][0, :, RH - 1].rearrange("b k v -> k b v"), Ssr[(RH - 1) % 2][:, :, :]
                         ).then_inc(s_retout, 16)
            DV.wait(sp, "S1.1")
            sp.dma_start(o[3][0, 0].rearrange("h k v -> k h v"), Sg[:, :, :]).then_inc(s_gdnout, 16)
            MM.wait(sp, "dS1.1")
            sp.dma_start(Ssg[:, :, :, :], d["state_gdn"][0].rearrange("b h k v -> k b h v")).then_inc(s_sgl, 16)
            sp.wait_ge(s_bt, 3)
            load_branch(2)
            for h in range(GH):
                if h == GH - 1:
                    sp.wait_ge(s_bt, 6)
                    load_branch(3)
                DS.wait(sp, f"S{h}")
                sp.dma_start(o[6][0, :, h].rearrange("b k v -> k b v"), Ssg[:, :, h, :]).then_inc(s_gsout, 16)
            sp.wait_ge(s_gsout, 16 * GH)
            for r in range(4, 6):
                sp.wait_ge(s_bt, 3 * (r - 2) + 3)
                load_branch(r)
            sp.wait_ge(s_bev, 4)
            sp.dma_start(wr[:, :, :], d["w_router"][0].rearrange("(k p) n -> p k n", p=P)).then_inc(s_wr, 16)
            sp.dma_start(br[:, :], d["b_router"]).then_inc(s_wr, 16)

            def load_gate_up(b, e, ks=range(KT), bias=True):
                src = d["w_gate_up"][0][e if isinstance(e, int) else bass.ds(e, 1)]
                if not isinstance(e, int):
                    src = src.rearrange("a n m -> (a n) m")
                for k in ks:
                    after(sp, m_guc, KT, b, k + 1 - KT)
                    sp.dma_start(gus[k][:, :], src[P * k:P * k + P, :]).then_inc(m_wgu[k], 16)
                if not bias:
                    return
                after(sp, m_gu, 1, b)
                sp.dma_start(bgu[:, :], d["b_gate_up"][0][bass.ds(e, 1), :]).then_inc(m_bgu, 16)

            def load_down(b, e):
                src = d["w_down"][0][e if isinstance(e, int) else bass.ds(e, 1)]
                if not isinstance(e, int):
                    src = src.rearrange("a n m -> (a n) m")
                for k in range(KT // 2):
                    after(sp, m_dc, KT // 2, b, k + 1 - KT // 2)
                    sp.dma_start(dns[k][:, :, :], src[2 * P * k:2 * P * k + 2 * P, :].rearrange(
                        "(a p) n -> p a n", p=P)).then_inc(m_wd[k], 16)
                after(sp, m_d, 1, b)
                sp.dma_start(bdn[:, :], d["b_down"][0][bass.ds(e, 1), :]).then_inc(m_bdn, 16)

            load_down(0, 0)
            load_gate_up(0, 0, range(6, 8), False)
            sp.wait_ge(s_bt, 15)
            load_gate_up(0, 0, range(2), False)
            sp.wait_ge(s_bt, 18)
            load_gate_up(0, 0, range(2, 4), False)
            rows = [a[0:DUMP, :].rearrange("(t a) n -> t (a n)", a=2) for a in (x2d, acc_d)]
            for n, t in ((1, X), (0, htok)):
                if t is X:
                    sp.wait_ge(s_res, 3)
                else:
                    sp.wait_ge(s_h, 6)
                sp.dma_start(rows[n][0:2 * P, :].rearrange("(c p) n -> p c n", p=P), t[:, 0:2, :]).then_inc(s_xd, 16)
                sp.dma_start(rows[n][2 * P:TOK, :], t[0:NB, 2, :]).then_inc(s_xd, 16)
            sp.wait_ge(s_xd, 64)
            sp.wait_ge(s_tr, 30)
            load_gate_up(0, 0, range(4, 6))
            load_gate_up(1, 1)
            load_gate_up(2, 2)
            load_down(1, 1)
            with sp.Fori(3, NE) as b:
                load_gate_up(b, b)
                load_down(b - 1, b - 1)
            load_down(NE - 1, NE - 1)

            def extra(j, b):
                e = sp.value_load(xei[0:1, bass.ds(j, 1)], min_val=0, max_val=NE - 1)
                load_gate_up(b, e)
                load_down(b, e)
            extra_blocks(sp, extra)
            sp.wait_ge(s_h, 6)
            sp.dma_start(WN[:, :], d["final_norm_w"].rearrange("(a n) -> a n", a=1).broadcast_to([P, D])
                         ).then_inc(s_wn, 16)
            sp.wait_ge(s_moe, 1)
            back = acc_d[0:DUMP, :].rearrange("(t a) n -> t (a n)", a=2)
            for c, r in TILES:
                sp.dma_start(X[0:r, c, :], back[P * c:P * c + r, :]).then_inc(s_back[c], 16)
            for c, r in TILES:
                sp.wait_ge(s_h, 7 + c)
                dst = o[0][0][P * c:P * c + P, :] if c < 2 else o[1].rearrange("b l n -> (b l) n")
                sp.dma_start(dst, htok[0:r, c, :]).then_inc(s_fin, 16)
            sp.wait_ge(s_fin, 48)
            sp.wait_ge(s_gdnout, 16)
            sp.wait_ge(s_retout, 80)

        @block.tensor
        def _(pe):
            def to_features(m, src, ready=None, uses={}, use=None, groups=range(5)):
                for i in groups:
                    n = 5 * m + i
                    if ready and i % 2 == 0:
                        pe.wait_ge(*ready[i // 2])
                    if n >= 2:
                        pe.wait_ge(s_trev, n - 1)
                    b = B[n % 2]
                    if i < 4:
                        for j in range(4):
                            k = 4 * (i % 2) + j
                            t = pe.transpose(b[:, P * j:P * j + P], src(i // 2)[:, P * k:P * k + P], ident)
                    else:
                        for k in range(KT):
                            t = pe.transpose(b[:, NB * k:NB * k + NB], src(2)[:, P * k:P * k + P],
                                             K[0:NB, C_ID:C_ID + NB])
                    t.then_inc(s_tr, 1)
                    if i in uses:
                        use(uses[i])

            pe.wait_ge(s_const, 16)
            pe.wait_ge(s_cwr, 16)
            pe.transpose(B[7][:, 0:4 * CCH], cwr[:, :], K[0:4 * CCH, C_ID:C_ID + 4 * CCH]).then_inc(s_cwT, 1)
            to_features(0, lambda c: htok[0:TILES[c][1], c, :], [(s_h, c + 1) for c in range(3)])
            pe.wait_ge(s_trev, 5)
            pe.wait_ge(s_wab, 16)
            for c, r in TILES:
                for k in range(KT):
                    t = pe.matmul(B[6][0:r, 2 * GH * c:2 * GH * c + 2 * GH], HT[:, k, P * c:P * c + r], wab[:, k, :],
                                  start=(k == 0), stop=(k == KT - 1))
            t.then_inc(s_ab, 1)

            with pe.Fori(0, 3) as i:
                for u in range(2):
                    pe.wait_ge(s_w[u], i * 16 + 16)
                    for m in range(4):
                        pe.wait_ge(s_raw, i * 8 + (4 * u + m + 1))
                        for k in range(KT):
                            t = pe.matmul(B[m % 2][:, 0:TOK], wslot[u][:, k, P * m:P * m + P], HT[:, k, :],
                                          start=(k == 0), stop=(k == KT - 1))
                        t.then_inc(s_ct, 1)

            pe.wait_ge(s_raw, CCH + 2)
            pe.wait_ge(s_hist, 16)
            pe.wait_ge(s_abev, 1)
            pe.wait_ge(s_cw, 1)
            for t2 in range(CCH):
                t = pe.transpose(B[t2 // 12][:, 24 * (t2 % 12):24 * (t2 % 12) + 24], hist[:, P * t2:P * t2 + P],
                                 K[0:24, C_ID:C_ID + 24])
            t.then_inc(s_hT, 1)
            for t2 in range(CCH):
                t = pe.transpose(B[2 + t2 // 4][0:11, P * (t2 % 4):P * (t2 % 4) + P], edges[:, t2, :], ident)
            t.then_inc(s_eT, 1)
            pe.wait_ge(s_eTev, 1)

            def decoding_tokens(lhsT, w, sbank, done):
                for k in range(KT):
                    for g in range(4):
                        t = pe.matmul(sbank[32 * g:32 * g + NB, 0:P], lhsT[:, k, 2 * P:TOK],
                                      w[:, k, P * g:P * g + P], start=(k == 0), stop=(k == KT - 1))
                t.then_inc(done, 1)

            def prompt_tokens(lhsT, w, banks, done):
                for c in range(2):
                    for k in range(KT):
                        t = pe.matmul(banks[c][:, :], lhsT[:, k, P * c:P * c + P], w[:, k, :],
                                      start=(k == 0), stop=(k == KT - 1))
                    t.then_inc(done, 1)

            def by_tokens(lhsT, w, banks, sbank, done):
                prompt_tokens(lhsT, w, banks, done)
                decoding_tokens(lhsT, w, sbank, done)

            def project(i):
                for u in range(2):
                    pe.wait_ge(s_w[u], i * 16 + 64)
                    pe.wait_ge(s_pfA, i * 2 + (u + 1))
                    pe.wait_ge(s_pfD, i * 2 + (u + 1))
                    by_tokens(HT, wslot[u], B[2 + 2 * u:4 + 2 * u], B[6 + u], s_pt)

            for i in range(2):
                project(i)
                pe.wait_ge(s_hTev, 1)
                pe.wait_ge(s_sq, i + 1)
                for t2 in range(GH * i, GH * i + GH):
                    if t2 >= 2:
                        pe.wait_ge(s_l2r, t2 - 1)
                    pe.matmul(B[t2 % 2][:, 0:TOK], ones, sq[:, t2, :], start=True, stop=True).then_inc(s_l2, 1)
            with pe.Fori(2, 6) as i:
                project(i)

            pe.wait_ge(s_rot, 3)
            pe.wait_ge(s_l2r, 2 * GH)
            to_features(1, lambda c: qkr[:, c, :] if c < 2 else qkrs[0:NB, :])
            pe.wait_ge(s_trev, 10)
            pe.wait_ge(s_pfA, 14)
            pe.wait_ge(s_pfD, 14)
            for c in range(2):
                for h in range(RH):
                    t = pe.matmul(B[2 + c][:, P * h:P * h + P], HT[:, RH + h, P * c:P * c + P],
                                  HT[:, h, P * c:P * c + P], start=True, stop=True)
                t.then_inc(s_in, 1)

            def vr(c, h):
                return Pt[:, c, D + RDV * h:D + RDV * h + RDV]

            def four(c, banks, lhsT, rhs):
                for h in range(RH):
                    t = pe.matmul(banks[h // 2][:, RDV * (h % 2):RDV * (h % 2) + RDV], lhsT(h), rhs(h),
                                  start=True, stop=True)
                t.then_inc(s_rm, 1)
            pe.wait_ge(s_kdr, 1)
            four(0, B[4:6], lambda h: kdr[:, 0, h, :], lambda h: vr(0, h))
            pe.wait_ge(s_inT, 1)
            four(0, B[6:8], lambda h: inT[:, 0, h, :], lambda h: vr(0, h))
            pe.wait_ge(s_Sr, 1)
            pe.wait_ge(s_inT, 2)
            four(1, B[2:4], lambda h: HT[:, h, P:2 * P], lambda h: Sr[:, h, :])
            pe.wait_ge(s_kdr, 2)
            four(1, B[4:6], lambda h: kdr[:, 1, h, :], lambda h: vr(1, h))
            pe.wait_ge(s_ro, 1)
            four(1, B[6:8], lambda h: inT[:, 1, h, :], lambda h: vr(1, h))
            pe.wait_ge(s_ro, 3)

            def decoded(h):
                pe.wait_ge(s_sup, h + 1)
                pe.wait_ge(s_qm, 1)
                for b in range(NB):
                    t = pe.matmul(B[6 + h // 2][0:NB, RDV * (h % 2):RDV * (h % 2) + RDV], qmr[:, h, b, :],
                                  Ssr[h % 2][:, b, :], start=(b == 0), stop=(b == NB - 1))
                t.then_inc(s_oc, 1)

            for h in range(RH):
                pe.wait_ge(s_km, h + 1)
                pe.wait_ge(s_Sr, 2)
                if h >= 1:
                    pe.wait_ge(s_sup, h)
                for b in range(NB):
                    t = pe.matmul(B[2 + b // 2][:, RDV * (b % 2):RDV * (b % 2) + RDV], kms[:, b, :],
                                  Ps[0:NB, D + RDV * h:D + RDV * h + RDV], start=True, stop=True)
                t.then_inc(s_out1, 1)
                if h >= 1:
                    decoded(h - 1)
            decoded(RH - 1)

            def heads(name, banks, f):
                for i in range(2):
                    for j in range(4):
                        t = f(banks[i][:, P * j:P * j + P], 4 * i + j)
                    MM.did(t, name(i))

            def prod(lhsT, rhs):
                return lambda out, h: pe.matmul(out, lhsT(h), rhs(h), start=True, stop=True)

            pe.wait_ge(s_osd, 1)
            pe.wait_ge(s_l2d, 2 * GH)
            for c in range(2):
                tk = slice(P * c, P * c + P)
                PL.wait(pe, f"gB.{c}")
                if c:
                    AC.wait(pe, "vn1.0")
                MM.did(pe.matmul(B[7][:, 0:GH], inc, gl[:, c, :], start=True, stop=True), f"G.{c}")
                if c:
                    DV.wait(pe, "O1.0")
                heads(lambda i: f"Gbc{i}.{c}", B[0:2], prod(lambda h: gB[:, h, :], lambda h: inc))
                PL.wait(pe, f"bB.{c}")
                heads(lambda i: f"Bbc{i}.{c}", B[2:4], prod(lambda h: tmpF[:, h, :], lambda h: ident))
                if c:
                    DV.wait(pe, "S1.0")
                heads(lambda i: f"KK{i}.{c}", B[4:6], prod(lambda h: uT[:, GH + h, tk], lambda h: uT[:, GH + h, tk]))
                DV.wait(pe, f"Gc.{c}")
                heads(lambda i: f"kT{i}.{c}", B[6:8], lambda out, h: pe.transpose(out, uT[:, GH + h, tk], ident))
                DV.wait(pe, f"D1.{c}")
                AC.wait(pe, f"eGl.{c}")
                DV.wait(pe, f"kd.{c}")
                heads(lambda i: f"QK{i}.{c}", B[0:2], prod(lambda h: uT[:, GH + h, tk], lambda h: uT[:, h, tk]))
                DV.wait(pe, f"dB1.{c}")
                heads(lambda i: f"vT{i}.{c}", B[2:4], lambda out, h: pe.transpose(out, uT[:, 2 * GH + h, tk], ident))
                DV.wait(pe, f"U1.{c}")
                heads(lambda i: f"T1{i}.{c}", B[4:6], lambda out, h: pe.transpose(out, U[:, h, :], ident))
                for lv in range(1, 7):
                    A = [Al0, Al1][lv % 2]
                    PL.wait(pe, f"Al{lv}.{c}")
                    for i in range(2):
                        if lv == 1:
                            AC.wait(pe, f"T{i}.{c}")
                            DV.wait(pe, f"kbG{i}.{c}" if c else f"kdg{i}.{c}")
                        else:
                            DV.wait(pe, f"T{lv - 1}.{i}.{c}")
                        for j in range(4):
                            h = 4 * i + j
                            t = pe.matmul(B[6 + i][:, P * j:P * j + P], A[:, h, :], T[:, h, :], start=True, stop=True)
                        MM.did(t, f"Y{lv}.{i}.{c}")
                    if lv < 6:
                        for i in range(2):
                            AC.wait(pe, f"Y{lv}.{i}.{c}")
                            DV.wait(pe, f"attn{i}.{c}" if lv == 1 else f"T{lv - 1}.{i}.{c}")
                            DV.wait(pe, f"U{i}.{c}" if lv == 1 else f"U{lv - 1}.{i}.{c}")
                            for j in range(4):
                                h = 4 * i + j
                                t = pe.matmul(B[i][:, P * j:P * j + P], U[:, h, :], Y[:, h, :], start=True, stop=True)
                            MM.did(t, f"dT{lv}.{i}.{c}")
                    for i in range(2):
                        AC.wait(pe, f"Y{lv}.{i}.{c}")
                        DV.wait(pe, f"bv{i}.{c}" if lv == 1 else f"U{lv - 1}.{i}.{c}")
                        for j in range(4):
                            h = 4 * i + j
                            t = pe.matmul(B[2 + i][:, P * j:P * j + P], Y[:, h, :], U[:, h, :], start=True, stop=True)
                        MM.did(t, f"dU{lv}.{i}.{c}")
                DV.wait(pe, f"U6.1.{c}")
                AC.wait(pe, f"Y6.1.{c}")
                if c:
                    heads(lambda i: f"wT{i}.{c}", B[4:6], prod(lambda h: kbG[:, h, :], lambda h: U[:, h, :]))
                    AC.wait(pe, "wT1.1")
                for i in range(2):
                    for j in range(4):
                        h = 4 * i + j
                        t = pe.matmul(B[6 + i][:, P * j:P * j + P], U[:, h, :], bv[:, h, :], start=True, stop=not c)
                        if c:
                            t = pe.matmul(B[6 + i][:, P * j:P * j + P], wTn[:, h, :], Sg[:, h, :],
                                          start=False, stop=True)
                    MM.did(t, f"u{i}.{c}")
                AC.wait(pe, f"vn1.{c}")
                DV.wait(pe, f"T5.1.{c}")
                heads(lambda i: f"o{i}.{c}", B[0:2], prod(lambda h: attnT[:, h, :], lambda h: vn[:, h, :]))
                if c:
                    heads(lambda i: f"qS{i}.{c}", B[2:4], prod(lambda h: uT[:, h, tk], lambda h: Sg[:, h, :]))
                AC.wait(pe, f"T1.{c}")
                heads(lambda i: f"dS{i}.{c}", B[4:6], prod(lambda h: kdg[:, h, :], lambda h: vn[:, h, :]))

            DV.wait(pe, "S1.1")
            sS = slice(2 * P, TOK)
            DS.wait(pe, "egd")
            MS.did(pe.matmul(B[7][:, 0:64], K[0:NB, C_ONE:C_ONE + P], egd[:, :, :].rearrange("p h b -> p (h b)"),
                             start=True, stop=True), "egb")
            for h in range(GH):
                t = pe.transpose(B[2 + h // 4][0:NB, P * (h % 4):P * (h % 4) + P], uT[:, GH + h, sS], ident)
            MS.did(t, "k")
            for h in range(GH):
                t = pe.transpose(B[4 + h // 4][0:NB, P * (h % 4):P * (h % 4) + P], uT[:, 2 * GH + h, sS], ident)
            MS.did(t, "v")

            def branch(r, between=None):
                pe.wait_ge(s_bw[r % 2], 16 * (r // 2) + 16)
                if r >= 2:
                    pe.wait_ge(s_bev, r - 1)
                f = OTb if r in (2, 3) else HT
                prompt_tokens(f, wslot[r % 2], B[2 + 2 * (r % 2):4 + 2 * (r % 2)], s_bt)
                if between:
                    between()
                decoding_tokens(f, wslot[r % 2], B[6 + r % 2], s_bt)

            to_features(2, lambda c: Prow(c)[:, 2 * D:3 * D], [(s_on, 1), (s_on, 2), (s_on, 3)])
            pe.wait_ge(s_trev, 15)
            DS.wait(pe, "ksm")
            branch(0)
            PS.wait(pe, "kmg")
            pe.wait_ge(s_sgl, 16)
            for i in range(2):
                for b in range(NB):
                    for j in range(4):
                        h = 4 * i + j
                        t = pe.matmul(B[0][32 * j:32 * j + NB, P * i:P * i + P], kmg[:, h, b, :], Ssg[:, b, h, :],
                                      start=(b == 0), stop=(b == NB - 1))
            MS.did(t, "kS")
            DS.wait(pe, "vsm")
            AS.wait(pe, "egb")
            pe.wait_ge(s_bw[1], 16)
            decoding_tokens(HT, wslot[1], B[7], s_bt)

            def decoded_g(h):
                DS.wait(pe, f"S{h}")
                if h == 4:
                    pe.wait_ge(s_bd, 1)
                for n in range(2):
                    for j in range(4):
                        b = 2 * j + n
                        t = pe.matmul(B[6 + h // 4][32 * j:32 * j + NB, P * (h % 4):P * (h % 4) + P],
                                      qmg[:, h, b, :], Ssg[:, b, h, :], start=(n == 0), stop=(n == 1))
                MS.did(t, f"oc{h}")

            for h in range(GH):
                PS.wait(pe, f"vm{h}")
                if h == 0:
                    pe.wait_ge(s_bev, 1)
                if h >= 2:
                    DS.wait(pe, f"S{h - 2}")
                for i in range(2):
                    t = pe.matmul(B[2 + 2 * (h % 2) + i][:, :], ksm[:, P * h:P * h + P],
                                  vm[h % 2][:, 4 * i:4 * i + 4, :].rearrange("p b n -> p (b n)"),
                                  start=True, stop=True)
                MS.did(t, f"out{h}")
                c = h // 4
                for k in range(2 * (h % 4), 2 * (h % 4) + 2):
                    t = pe.matmul(B[c][:, :], HT[:, k, P * c:P * c + P], wslot[1][:, k, :],
                                  start=(k == 0), stop=(k == KT - 1))
                if h % 4 == 3:
                    t.then_inc(s_bt, 1)
                if h >= 1:
                    decoded_g(h - 1)
            decoded_g(GH - 1)

            pe.wait_ge(s_bev, 2)
            def turn(m, col, ready, groups):
                to_features(m, lambda c: Prow(c)[:, col:col + D], ready, groups=groups)
                pe.wait_ge(s_trev, 5 * m + groups[-1] + 1)

            pe.wait_ge(s_bev, 2)
            for r in range(2, 6):
                if r == 2:
                    use = (3, Z0, [(s_on, 4), (s_on, 5), (s_on, 6)])
                elif r == 4:
                    use = (4, GA0, [(s_mix, 4), (s_mix, 5), (s_mix, 6)])
                if r % 2 == 0:
                    turn(*use, range(4))
                    DS.wait(pe, f"S{GH - 1}")
                    branch(r, lambda: turn(*use, range(4, 5)))
                else:
                    branch(r)

            def route(c):
                r = TILES[c][1]
                pe.wait_ge(s_trev, min(27 + 2 * c, 30))
                if c == 0:
                    pe.wait_ge(s_wr, 32)
                    pe.wait_ge(s_bev, 5)
                out = B[2][0:r, NE * c:NE * c + NE]
                for k in range(KT):
                    pe.matmul(out, HT[:, k, P * c:P * c + r], wr[:, k, :], start=(k == 0), stop=False)
                pe.matmul(out, K[0:1, C_ONE:C_ONE + r], br[:, :], start=False, stop=True).then_inc(s_lg, 1)

            to_features(5, lambda c: htok[0:TILES[c][1], c, :], [(s_h, c + 4) for c in range(3)], {3: 0, 4: 1}, route)
            route(2)
            pe.wait_ge(s_sel, 1)
            for c, r in TILES:
                out = B[3][0:r, NE * c:NE * c + NE]
                for c2 in range(c):
                    pe.matmul(out, K[:, C_ONE:C_ONE + r], sel[:, c2, :], start=(c2 == 0), stop=False)
                pe.matmul(out, K[0:r, C_INC:C_INC + r], sel[0:r, c, :], start=(c == 0), stop=True)
            for c, r in TILES:
                t = pe.matmul(B[3][:, 3 * NE:4 * NE], K[0:r, C_ONE:C_ONE + P], sel[0:r, c, :],
                              start=(c == 0), stop=(c == 2))
            t.then_inc(s_pos, 1)

            def slots(b):
                after(pe, m_O, 1, b, 1)
                after(pe, m_v, 1, b)
                for c, r in TILES:
                    t = pe.matmul(B[5][:, 0:2], O[0:r, c, :], tw[0:r, c, :], start=(c == 0), stop=(c == 2))
                t.then_inc(m_im, 1)

            def turn_x(b):
                after(pe, m_g, 16, b, 16)
                after(pe, m_txev, 1, b)
                for j in range(4):
                    t = pe.transpose(B[4][:, P * j:P * j + P], xg[:, P * j:P * j + P], ident)
                t.then_inc(m_tx, 1)

            def gate_up(b):
                after(pe, m_txev, 1, b, 1)
                after(pe, m_gl, 1, b)
                for k in range(KT):
                    after(pe, m_wgu[k], 16, b, 16)
                    for part in range(2):
                        for g in range(2):
                            t = pe.matmul(B[part][64 * g:64 * g + 64, :], xT[:, k % 4, 64 * (k // 4):64 * (k // 4) + 64],
                                          gus[k][:, D * part + 512 * g:D * part + 512 * g + 512],
                                          start=(k == 0), stop=False)
                    t.then_inc(m_guc, 1)
                after(pe, m_bgu, 16, b, 16)
                for part in range(2):
                    for g in range(2):
                        t = pe.matmul(B[part][64 * g:64 * g + 64, :], K[0:1, C_ONE:C_ONE + 64],
                                      bgu[:, D * part + 512 * g:D * part + 512 * g + 512], start=False, stop=True)
                t.then_inc(m_gu, 1)

            def turn_act(b):
                after(pe, m_act, 1, b, 1)
                after(pe, m_taev, 1, b)
                for j in range(4):
                    t = pe.transpose(B[2][:, P * j:P * j + P], ac[:, P * j:P * j + P], ident)
                t.then_inc(m_ta, 1)

            def down(b):
                after(pe, m_taev, 1, b, 1)
                after(pe, m_yev, 1, b)
                for k in range(KT):
                    if k % 2 == 0:
                        after(pe, m_wd[k // 2], 16, b, 16)
                    for g in range(2):
                        t = pe.matmul(B[3][64 * g:64 * g + 64, :], acT[:, k % 4, 64 * (k // 4):64 * (k // 4) + 64],
                                      dns[k // 2][:, k % 2, 512 * g:512 * g + 512], start=(k == 0), stop=False)
                    if k % 2:
                        t.then_inc(m_dc, 1)
                after(pe, m_bdn, 16, b, 16)
                for g in range(2):
                    t = pe.matmul(B[3][64 * g:64 * g + 64, :], K[0:1, C_ONE:C_ONE + 64],
                                  bdn[:, 512 * g:512 * g + 512], start=False, stop=True)
                t.then_inc(m_d, 1)

            pe.wait_ge(s_tab, 1)
            slots(0)
            turn_x(0)
            slots(1)
            gate_up(0)
            turn_x(1)
            slots(2)
            def step(b):
                gate_up(b)
                turn_act(b - 1)
                turn_x(b + 1)
                down(b - 1)
                slots(b + 2)

            step(1)
            with pe.Fori(2, NE - 2) as b:
                step(b)
            gate_up(NE - 2)
            turn_act(NE - 3)
            turn_x(NE - 1)
            down(NE - 3)
            gate_up(NE - 1)
            turn_act(NE - 2)
            down(NE - 2)
            turn_act(NE - 1)
            down(NE - 1)

            def extra(j, b):
                slots(b)
                turn_x(b)
                gate_up(b)
                turn_act(b)
                down(b)
            extra_blocks(pe, extra)

        @block.scalar
        def _(act):
            link = chain(act, act_chain)
            act.sem_inc(s_raw, 2)
            act.sem_inc(s_pfA, 2)

            def squares(n, arrived=None):
                for c, r in TILES:
                    if arrived:
                        act.wait_ge(arrived[c], 16)
                    nc.scalar.activation(htok[0:r, c, :], X[0:r, c, :], ACT.Square,
                                         accum_out=ss[0:r, c:c + 1]).then_inc(s_ss, 1)
                act.wait_ge(s_ss, 3 * n + 3)
                nc.scalar.activation(rs[:, :], ss[:, :], ACT.Sqrt, bias=eps[:, :], scale=1.0 / D).then_inc(s_rs, 1)

            def to_features(m, dst, groups=range(5)):
                for i in groups:
                    n = 5 * m + i
                    act.wait_ge(s_tr, n + 1)
                    if i < 4:
                        g, c = i % 2, i // 2
                        nc.scalar.copy(dst[:, 4 * g:4 * g + 4, P * c:P * c + P], quad(B[n % 2])).then_inc(s_trev, 1)
                    else:
                        nc.scalar.copy(dst[:, :, 2 * P:TOK],
                                       B[n % 2][:, 0:KT * NB].rearrange("p (k b) -> p k b", k=KT)).then_inc(s_trev, 1)

            act.wait_ge(s_init, 1)
            squares(0, s_x)
            to_features(0, HT)
            act.wait_ge(s_gv, 1)
            act.wait_ge(s_prm, 48)
            nc.scalar.activation(gt2[:, :, :], gt1[:, :, :], ACT.Exp, scale=-1.0).then_inc(s_ga, 1)
            nc.scalar.activation(prm[:, 0, :], prm[:, 0, :], ACT.Exp).then_inc(s_ga, 1)
            act.wait_ge(s_ga, 2)
            nc.scalar.activation(gt2[:, :, :], gt2[:, :, :], ACT.Ln, bias=K[:, C_ONE:C_ONE + 1]).then_inc(s_ga, 1)
            nc.scalar.activation(beta[:, :, :], gts[:, :, GH:2 * GH], ACT.Sigmoid).then_inc(s_ga, 1)
            with act.Fori(0, 3) as i:
                for m in range(8):
                    act.wait_ge(s_ct, i * 8 + (m + 1))
                    act.wait_ge(s_cv, i * 8 + (m + 1))
                    nc.scalar.copy(raw[:, m % 2, 3:259], B[m % 2][:, 0:256])
                    nc.scalar.copy(edges[:, bass.ds(i * 8 + m, 1), :],
                                   B[m % 2][:, 253:264].unsqueeze(1)).then_inc(s_raw, 1)

            act.wait_ge(s_cv, CCH + 2)
            act.wait_ge(s_sconv, 1)
            for i in range(3):
                f = uT[:, GH * i:GH * i + GH, :]
                nc.scalar.activation(f, f, ACT.Silu).then_inc(s_silu, 1)
            for i in range(6):
                for u in range(2):
                    col = i * 1024 + 512 * u
                    act.wait_ge(s_pt, i * 6 + (3 * u + 1))
                    nc.scalar.copy(Pt[:, 0, col:col + 512], B[2 + 2 * u][:, :])
                    act.wait_ge(s_pt, i * 6 + (3 * u + 3))
                    for g in range(4):
                        t = nc.scalar.copy(Ps[0:NB, col + P * g:col + P * g + P], B[6 + u][32 * g:32 * g + NB, 0:P])
                    t.then_inc(s_pfA, 1)
                if i < 2:
                    for t2 in range(GH * i, GH * i + GH):
                        act.wait_ge(s_l2, t2 + 1)
                        nc.scalar.activation(sq[:, t2, :], B[t2 % 2][:, 0:TOK], ACT.Sqrt, bias=eps[:, :]
                                             ).then_inc(s_l2r, 1)
                if i in (2, 3):
                    act.wait_ge(s_pfA, 2 * i + 4)
                    act.wait_ge(s_pfD, 2 * i + 4)
                    for c, r in TILES:
                        f = Prow(c)[:, D * i:D * i + D]
                        nc.scalar.activation(f, f, ACT.Silu).then_inc(s_sg, 1)
            to_features(1, HT)
            act.wait_ge(s_rm, 1)
            for i in range(2):
                t = nc.scalar.copy(Sr[:, 2 * i:2 * i + 2, :], B[4 + i][:, :].rearrange("p (h n) -> p h n", h=2))
            t.then_inc(s_Sr, 1)
            act.wait_ge(s_pfA, 14)
            act.wait_ge(s_pfD, 14)
            for c, r in TILES:
                f = Prow(c)[:, GA0:GA0 + 2 * D]
                nc.scalar.activation(f, f, ACT.Sigmoid).then_inc(s_sig, 1)

            def head_norms(n, width, hds):
                c, r = TILES[n % 3]
                act.wait_ge(s_hss, n + 1)
                nc.scalar.activation(rr[0:r, c, 0:hds], rr[0:r, c, 0:hds], ACT.Sqrt, bias=eps[0:r, :],
                                     scale=1.0 / width).then_inc(s_hrt, 1)
            for n in range(2):
                head_norms(n, RDV, RH)
            for c in range(2):
                DV.wait(act, f"Gc.{c}")
                if c:
                    DV.wait(act, "S1.0")
                AC.did(nc.scalar.activation(eG[:, :], Gc[:, :], ACT.Exp), f"eG.{c}")
                DV.wait(act, f"kd.{c}")
                for i in range(2):
                    t = nc.scalar.activation(eGl[:, 4 * i:4 * i + 4], quad(B[i])[:, :, P - 1:P].rearrange(
                        "p a b -> p (a b)"), ACT.Exp)
                AC.did(t, f"eGl.{c}")
                AC.did(nc.scalar.activation(kds[:, :], kds[:, :], ACT.Exp), f"kds.{c}")
                DV.wait(act, f"min.{c}")
                AC.did(nc.scalar.activation(DT[:, :, :], DT[:, :, :], ACT.Exp), f"exp.{c}")
                for i in range(2):
                    MM.wait(act, f"T1{i}.{c}")
                    AC.did(nc.scalar.copy(half(T, i), quad(B[4 + i])), f"T{i}.{c}")
                for lv in range(1, 7):
                    for i in range(2):
                        MM.wait(act, f"Y{lv}.{i}.{c}")
                        if lv > 1:
                            MM.wait(act, f"dU{lv - 1}.{i}.{c}")
                        AC.did(nc.scalar.copy(half(Y, i), quad(B[6 + i])), f"Y{lv}.{i}.{c}")
                    if lv == 4:
                        head_norms(3, P, GH) if c else head_norms(2, RDV, RH)
                if c:
                    for i in range(2):
                        MM.wait(act, f"wT{i}.{c}")
                        AC.did(nc.scalar.mul(half(wTn, i), quad(B[4 + i]), -1.0), f"wT{i}.{c}")
                for i in range(2):
                    MM.wait(act, f"u{i}.{c}")
                    AC.did(nc.scalar.copy(half(vn, i), quad(B[6 + i])), f"vn{i}.{c}")
            DS.wait(act, "eg")
            AS.did(nc.scalar.activation(gt1[0:NB, 2, :], gl[0:NB, 2, :], ACT.Exp), "eg")
            MS.wait(act, "egb")
            AS.did(nc.scalar.copy(egb[:, :], B[7][:, 0:64]), "egb")
            to_features(2, HT)
            head_norms(4, P, GH)
            to_features(3, OTb, range(4))
            head_norms(5, P, GH)
            to_features(3, OTb, range(4, 5))
            to_features(4, HT)
            for first, last in ((0, 1), (1, 3)):
                for c, r in TILES[first:last]:
                    act.wait_ge(s_res, c + 1)
                    nc.scalar.activation(htok[0:r, c, :], X[0:r, c, :], ACT.Square,
                                         accum_out=ss[0:r, c:c + 1]).then_inc(s_ss, 1)
                act.wait_ge(s_ss, 3 + last)
                nc.scalar.activation(rs[:, first:last], ss[:, first:last], ACT.Sqrt, bias=eps[:, :], scale=1.0 / D
                                     ).then_inc(s_rs, 1)
            to_features(5, HT)
            act.wait_ge(s_exd, 1)
            nc.scalar.activation(ex[:, :, :], ex[:, :, :], ACT.Exp).then_inc(s_ex, 1)

            def x_out(b):
                after(act, m_tx, 1, b, 1)
                nc.scalar.copy(xT[:, :, :], quad(B[4])).then_inc(m_txev, 1)

            def sigmoid(b):
                after(act, m_glu, 1, b, 1)
                after(act, m_act, 1, b)
                nc.scalar.activation(sg[:, :], glu[:, :], ACT.Sigmoid, scale=1.702).then_inc(m_sig, 1)

            def act_out(b):
                after(act, m_ta, 1, b, 1)
                nc.scalar.copy(acT[:, :, :], quad(B[2])).then_inc(m_taev, 1)

            def y_out(b):
                after(act, m_d, 1, b, 1)
                after(act, m_s, 16, b)
                w = vt[:, b, 1:2] if isinstance(b, int) else vt[:, bass.ds(b, 1), 1:2].rearrange("p a n -> p (a n)")
                nc.scalar.activation(yb[:, :], B[3][:, :], ACT.Copy, scale=w).then_inc(m_yev, 1)

            x_out(0)
            x_out(1)
            sigmoid(0)
            def step(b):
                act_out(b - 1)
                x_out(b + 1)
                sigmoid(b)
                y_out(b - 1)

            step(1)
            with act.Fori(2, NE - 2) as b:
                step(b)
            act_out(NE - 3)
            x_out(NE - 1)
            sigmoid(NE - 2)
            y_out(NE - 3)
            act_out(NE - 2)
            sigmoid(NE - 1)
            y_out(NE - 2)
            act_out(NE - 1)
            y_out(NE - 1)

            def extra(j, b):
                x_out(b)
                sigmoid(b)
                act_out(b)
                y_out(b)
            extra_blocks(act, extra)
            squares(2, s_back)

        @block.gpsimd
        def _(pool):
            link = chain(pool, pool_chain)
            g = nc.gpsimd
            new_s = uT[:, :, 2 * P:TOK]
            hb = histT[:, :, :].rearrange("p t (b i) -> p t b i", i=3)
            tmp = at("sconv_tmp", scr + 24576, [P, CCH, NB])
            pool.wait_ge(s_cw, 1)
            pool.wait_ge(s_raw, CCH + 2)
            link(g.tensor_tensor(new_s, edges[:, :, 3:11], cw[:, :, 3:4].broadcast_to([P, CCH, NB]), ALU.mult))
            pool.wait_ge(s_hTev, 1)
            for i in range(3):
                link(g.tensor_tensor(tmp[:, :, :], hb[:, :, :, i], cw[:, :, i:i + 1].broadcast_to([P, CCH, NB]),
                                     ALU.mult))
                t = g.tensor_tensor(new_s, new_s, tmp[:, :, :], ALU.add)
                if i < 2:
                    link(t)
            t.then_inc(s_sconv, 1)
            pool.wait_ge(s_eTev, 1)
            pool.dma_start(o[4][0, 0], ctok[0:3, :]).then_inc(s_out, 16)
            pool.dma_start(o[7][0, :, 2, :], ctok[3:11, :]).then_inc(s_out, 16)
            pool.dma_start(o[7][0, :, 0:2, :], d["state_conv"][0, :, 1:3, :]).then_inc(s_out, 16)
            pool.wait_ge(s_hT, 1)
            for i in range(2):
                pool.wait_ge(s_silu, i + 1)
                f = uT[:, GH * i:GH * i + GH, :]
                g.tensor_tensor(sq[:, GH * i:GH * i + GH, :], f, f, ALU.mult).then_inc(s_sq, 1)
            pool.wait_ge(s_tables, 16)
            for c in range(2):
                pool.wait_ge(s_rot, c + 1)
                g.tensor_tensor(kdr[:, c, :, :], qkr[:, c, 512:D].rearrange("p (h n) -> p h n", h=RH),
                                K[:, C_KD:C_KD + RH].unsqueeze(2).broadcast_to([P, RH, P]), ALU.mult).then_inc(s_kdr, 1)
            for h in range(RH):
                if h == 0:
                    pool.wait_ge(s_tr, 10)
                    pool.wait_ge(s_kdr, 2)
                    pool.wait_ge(s_rot, 3)
                if h >= 1:
                    pool.wait_ge(s_out1, h)
                g.tensor_tensor(kms[:, :, :], bc(qkrs[0:NB, 512 + P * h:512 + P * h + P], NB, 1),
                                bc(K[0:NB, C_ID:C_ID + NB], P, 2), ALU.mult).then_inc(s_km, 1)
                if h == 0:
                    pool.wait_ge(s_trev, 10)
                    for j in range(RH):
                        t = g.tensor_tensor(qmr[:, j], bc(HT[:, j, 2 * P:TOK], NB), diag, ALU.mult)
                    t.then_inc(s_qm, 1)
            pool.wait_ge(s_l2d, 2 * GH)
            pool.wait_ge(s_cv, CCH + 2)
            for n, f in (("qmg", qmg), ("kmg", kmg)):
                for h in range(GH):
                    t = g.tensor_tensor(f[:, h], bc(uT[:, (GH if n == "kmg" else 0) + h, 2 * P:TOK], NB), diag, ALU.mult)
                PS.did(t, n)
            pool.wait_ge(s_gv, 2)
            pool.wait_ge(s_rm, 5)
            pool.wait_ge(s_out1, RH)
            for c in range(2):
                if c:
                    MM.wait(pool, "Gbc1.0")
                PL.did(g.tensor_copy(gB[:, :, :], bc(gl[:, c, :], P, 2)), f"gB.{c}")
                if c:
                    DV.wait(pool, "At1.0")
                PL.did(g.tensor_copy(tmpF[:, :, :], bc(beta[:, c, :], P, 2)), f"bB.{c}")
                for lv in range(7):
                    if lv == 0:
                        DV.wait(pool, f"At1.{c}")
                        if c:
                            MM.wait(pool, "dU6.1.0")
                    elif lv == 2:
                        DV.wait(pool, f"U1.{c}")
                    elif lv > 2:
                        MM.wait(pool, f"Y{lv - 2}.1.{c}")
                    A = [Al0, Al1][lv % 2]
                    PL.did(g.tensor_tensor(A[:, :, :], At[:, :, :],
                                           bc(K[:, C_LVL + P * lv:C_LVL + P * lv + P], GH, 1), ALU.mult), f"Al{lv}.{c}")
            pool.wait_ge(s_out, 48)
            DS.wait(pool, "vn3")
            for h in range(GH):
                if h >= 2:
                    MS.wait(pool, f"out{h - 2}")
                PS.did(g.tensor_tensor(vm[h % 2][:, :, :], bc(vsm[:, P * h:P * h + P], NB, 1),
                                       bc(K[0:NB, C_ID:C_ID + NB], P, 2), ALU.mult), f"vm{h}")
            pool.wait_ge(s_zr, 1)
            pool.dma_start(x2d[DUMP:ROWS, :], zrow[:, :]).then_inc(s_zd, 16)
            pool.dma_start(acc_d[DUMP:ROWS, :], zrow[:, :]).then_inc(s_zd, 16)
            pool.wait_ge(s_zd, 32)
            pool.wait_ge(s_xd, 64)

            def gather(b):
                after(pool, m_gi, 1, b, 1)
                after(pool, m_tx, 1, b)
                pool.sem_inc(m_go)
                pool.indirect_dma_start(xg[:, :], None, x2d, bass.IndirectOffsetOnAxis(ap=gidx[:, 0:1], axis=0)
                                        ).then_inc(m_g, 16)

            def scatter(b):
                after(pool, m_yev, 1, b, 1)
                after(pool, m_si, 1, b, 1)
                after(pool, m_s, 16, b)
                pool.sem_inc(m_go)
                pool.indirect_dma_start(acc_d, bass.IndirectOffsetOnAxis(ap=sidx[:, 0:1], axis=0), yb[:, :], None,
                                        compute_op=ALU.add).then_inc(m_s, 16)

            gather(0)
            gather(1)
            gather(2)
            def step(b):
                scatter(b - 1)
                gather(b + 2)

            step(1)
            with pool.Fori(2, NE - 2) as b:
                step(b)
            for b in range(NE - 3, NE):
                scatter(b)
            pool.wait_ge(m_s, 16 * NE)

            def extra(j, b):
                gather(b)
                scatter(b)
                after(pool, m_s, 16, b, 16)
            extra_blocks(pool, extra)
            pool.sem_inc(s_moe, 1)

        @block.vector
        def _(dve):
            link = chain(dve, dve_chain)
            v = nc.vector
            dve.sem_inc(s_cv, 2)
            dve.sem_inc(s_pfD, 2)
            v.memset(raw[:, :, 0:3], 0.0)
            v.memset(eps[:, :], EPS)
            v.memset(ss[:, :], 1.0).then_inc(s_init, 1)

            def normed(n):
                dve.wait_ge(s_rs, 4 if n else 1)
                link(v.reciprocal(rs[:, :], rs[:, :]))
                dve.wait_ge(s_wn, 16 * n + 16)
                for c, r in TILES:
                    v.scalar_tensor_tensor(htok[0:r, c, :], X[0:r, c, :], rs[0:r, c:c + 1], WN[0:r, :],
                                           ALU.mult, ALU.mult).then_inc(s_h, 1)

            for c in range(3):
                dve.wait_ge(s_x[c], 16)
            normed(0)
            dve.wait_ge(s_cwT, 1)
            v.tensor_copy(cw[:, :, :], B[7][:, 0:4 * CCH].rearrange("p (i c) -> p c i", i=4)).then_inc(s_cw, 1)
            link(v.memset(gts[:, :, :], 0.0))
            dve.wait_ge(s_ab, 1)
            for c, r in TILES:
                t = v.tensor_copy(gts[0:r, c, :], B[6][0:r, 2 * GH * c:2 * GH * c + 2 * GH])
            t.then_inc(s_abev, 1)
            dve.wait_ge(s_abev, 1)
            dve.wait_ge(s_prm, 48)
            ta = gts[:, :, 0:GH]
            link(v.tensor_tensor(ta, ta, bc(prm[:, 1, :], 3, 1), ALU.add))
            link(v.tensor_scalar(gt2[:, :, :], ta, -1.0, None, ALU.mult))
            v.tensor_tensor(gt1[:, :, :], ta, gt2[:, :, :], ALU.max).then_inc(s_gv, 1)
            dve.wait_ge(s_ga, 3)
            link(v.scalar_tensor_tensor(gt2[:, :, :], ta, 0.0, gt2[:, :, :], ALU.max, ALU.add))
            v.scalar_tensor_tensor(gl[:, :, :], gt2[:, :, :], -1.0, bc(prm[:, 0, :], 3, 1), ALU.mult, ALU.mult
                                   ).then_inc(s_gv, 1)
            dve.wait_ge(s_cw, 1)
            with dve.Fori(0, 3) as i:
                for m in range(8):
                    dve.wait_ge(s_raw, i * 8 + (m + 3))
                    t = i * 8 + m
                    acc = uT[:, bass.ds(t, 1), 0:256].rearrange("p a n -> p (a n)")

                    def tap(j):
                        return cw[:, bass.ds(t, 1), j:j + 1].rearrange("p a n -> p (a n)")
                    v.tensor_scalar(acc, raw[:, m % 2, 0:256], tap(0), None, ALU.mult).then_inc(s_cvc, 1)
                    for j in range(1, 4):
                        dve.wait_ge(s_cvc, i * 24 + (3 * m + j))
                        v.scalar_tensor_tensor(acc, raw[:, m % 2, j:j + 256], tap(j), acc, ALU.mult, ALU.add
                                               ).then_inc(s_cvc if j < 3 else s_cv, 1)
            for i in range(2):
                dve.wait_ge(s_hT, 1)
                t = v.tensor_copy(histT[:, 12 * i:12 * i + 12, :], B[i][:, 0:288].rearrange("p (t n) -> p t n", t=12))
            t.then_inc(s_hTev, 1)
            dve.wait_ge(s_eT, 1)
            for i in range(6):
                t = v.tensor_copy(ctok[:, 512 * i:512 * i + 512], B[2 + i][0:11, :])
            t.then_inc(s_eTev, 1)
            def evac(i):
                for u in range(2):
                    dve.wait_ge(s_pt, i * 6 + (3 * u + 2))
                    v.tensor_copy(Pt[:, 1, bass.ds(i * 1024 + 512 * u, 512)], B[3 + 2 * u][:, :]).then_inc(s_pfD, 1)

            for i in range(2):
                evac(i)
                for t2 in range(GH * i, GH * i + GH):
                    dve.wait_ge(s_l2r, t2 + 1)
                    link(v.reciprocal(sq[:, t2, :], sq[:, t2, :]))
                    v.scalar_tensor_tensor(uT[:, t2, :], sq[:, t2, :], P ** -0.5 if t2 < GH else 1.0, uT[:, t2, :],
                                           ALU.mult, ALU.mult).then_inc(s_l2d, 1)
            evac(2)
            dve.wait_ge(s_l2d, 2 * GH)
            dve.wait_ge(s_out, 48)
            dve.wait_ge(s_tables, 16)
            dve.wait_ge(s_pfA, 4)
            dve.wait_ge(s_pfD, 4)
            for c, r in TILES:
                for qk in range(2):
                    src = Prow(c)[:, 512 * qk:512 * qk + 512].rearrange("p (h e n) -> p h e n", h=RH, e=2)
                    dst = (qkr[:, c, :] if c < 2 else qkrs[0:NB, :])[:, 512 * qk:512 * qk + 512].rearrange(
                        "p (h e n) -> p h e n", h=RH, e=2)

                    def trig(cs):
                        f = C_TRIG + ((c * 2 + cs) * 2 + qk) * 64
                        return bc(K[0:r, f:f + 64], RH, 1)
                    v.tensor_tensor(rt[0:r, 0], src[:, :, 0, :], trig(0), ALU.mult)
                    v.tensor_tensor(rt[0:r, 1], src[:, :, 1, :], trig(1), ALU.mult)
                    v.tensor_tensor(rt[0:r, 2], src[:, :, 0, :], trig(1), ALU.mult)
                    link(v.tensor_tensor(rt[0:r, 3], src[:, :, 1, :], trig(0), ALU.mult))
                    v.tensor_tensor(dst[:, :, 0, :], rt[0:r, 0], rt[0:r, 1], ALU.subtract)
                    t = v.tensor_tensor(dst[:, :, 1, :], rt[0:r, 2], rt[0:r, 3], ALU.add)
                    if qk == 0:
                        link(t)
                    else:
                        t.then_inc(s_rot, 1)
                dve.wait_ge(s_rot, c + 1)
            with dve.Fori(3, 6) as i:
                evac(i)
            for c in range(2):
                dve.wait_ge(s_in, c + 1)
                v.tensor_tensor(inT[:, c], quad(B[2 + c]), K[:, C_DM:C_DM + 512].rearrange("p (h n) -> p h n", h=RH),
                                ALU.mult).then_inc(s_inT, 1)
            dve.wait_ge(s_rm, 2)
            for i in range(2):
                t = v.tensor_copy(Pt[:, 0, 512 * i:512 * i + 512], B[6 + i][:, :])
            t.then_inc(s_ro, 1)
            dve.wait_ge(s_rm, 4)
            dve.wait_ge(s_Sr, 1)
            for h in range(RH):
                t = v.scalar_tensor_tensor(Sr[:, h, :], Sr[:, h, :], float(np.exp(P * LOGG[h])),
                                           B[4 + h // 2][:, RDV * (h % 2):RDV * (h % 2) + RDV], ALU.mult, ALU.add)
            t.then_inc(s_Sr, 1)
            dve.wait_ge(s_rm, 5)
            for h in range(RH):
                cols = slice(RDV * (h % 2), RDV * (h % 2) + RDV)
                t = v.tensor_scalar(Pt[:, 1, RDV * h:RDV * h + RDV], B[2 + h // 2][:, cols],
                                    K[:, C_QD + h:C_QD + h + 1], None, ALU.mult)
            t.then_inc(s_ro, 1)
            dve.wait_ge(s_ro, 2)
            for i in range(2):
                f = Pt[:, 1, 512 * i:512 * i + 512]
                t = v.tensor_tensor(f, f, B[6 + i][:, :], ALU.add)
            t.then_inc(s_ro, 1)
            def head_step(step, n, x3, t3, gate, hds, weight=None):
                c, r = TILES[n % 3]
                w = D // hds
                g3 = gate.rearrange("p (h n) -> p h n", h=hds)
                if step == 0:
                    link(v.tensor_tensor(t3, x3, x3, ALU.mult))
                elif step == 1:
                    v.tensor_reduce(rr[0:r, c, 0:hds], t3, AX.X, ALU.add).then_inc(s_hss, 1)
                elif step == 2 and weight is not None:
                    link(v.tensor_tensor(g3, g3, bc(weight, hds, 1), ALU.mult))
                elif step == 3:
                    dve.wait_ge(s_hrt, n + 1)
                    link(v.reciprocal(rr[0:r, c, 0:hds], rr[0:r, c, 0:hds]))
                    link(v.tensor_tensor(t3, x3, bc(rr[0:r, c, 0:hds], w, 2), ALU.mult))
                elif step == 4:
                    v.tensor_tensor(g3, g3, t3, ALU.mult).then_inc(s_on, 1)
                    dve.wait_ge(s_on, n + 1)

            def head_out(*args):
                for step in range(5):
                    head_step(step, *args)

            def by_head(f, hds):
                return f.rearrange("p (h n) -> p h n", h=hds)

            def retention_out(c, r):
                head_out(c, by_head(Prow(c)[:, 0:D], RH), by_head(sqr[0:r, :], RH), Prow(c)[:, 2 * D:3 * D], RH)

            dve.wait_ge(s_ro, 3)
            dve.wait_ge(s_sg, 3)
            for h in range(RH):
                dve.wait_ge(s_out1, h + 1)
                dve.wait_ge(s_sr[h % 2], 16 * (h // 2) + 16)
                for i in range(4):
                    f = Ssr[h % 2][:, 2 * i:2 * i + 2, :]
                    t = v.scalar_tensor_tensor(f, f, float(np.exp(LOGG[h])), B[2 + i][:, :].rearrange(
                        "p (b n) -> p b n", b=2), ALU.mult, ALU.add)
                t.then_inc(s_sup, 1)
                if h < 2:
                    retention_out(h, P)
            dve.wait_ge(s_oc, RH)
            for i in range(2):
                t = v.tensor_copy(Ps[0:NB, 512 * i:512 * i + 512], B[6 + i][0:NB, :])
            t.then_inc(s_osd, 1)

            dve.wait_ge(s_sg, 6)

            def halves(name, f):
                for i in range(2):
                    DV.did(f(i), name(i))

            for c in range(2):
                MM.wait(dve, f"G.{c}")
                DV.did(v.tensor_copy(Gc[:, :], B[7][:, 0:GH]), f"Gc.{c}")
                DV.wait(dve, f"Gc.{c}")
                for i in range(2):
                    MM.wait(dve, f"Gbc{i}.{c}")
                    DV.did(v.tensor_tensor(half(DT, i), quad(B[i]), bc(Gc[:, 4 * i:4 * i + 4], P, 2), ALU.subtract),
                           f"D{i}.{c}")
                for i in range(2):
                    t = v.tensor_tensor(kds[:, 4 * i:4 * i + 4].unsqueeze(2), quad(B[i])[:, :, P - 1:P],
                                        Gc[:, 4 * i:4 * i + 4].unsqueeze(2), ALU.subtract)
                DV.did(t, f"kd.{c}")
                DV.wait(dve, f"D1.{c}")
                DV.did(v.tensor_scalar(DT[:, :, :], DT[:, :, :], 0.0, None, ALU.min), f"min.{c}")
                AC.wait(dve, f"exp.{c}")
                DV.did(v.tensor_tensor(DT[:, :, :], DT[:, :, :], bc(inc, GH, 1), ALU.mult), f"mask.{c}")
                DV.wait(dve, f"mask.{c}")
                MM.wait(dve, f"Bbc1.{c}")
                PL.wait(dve, f"bB.{c}")
                halves(lambda i: f"dB{i}.{c}",
                       lambda i: v.tensor_tensor(half(tmpF, i), half(DT, i), quad(B[2 + i]), ALU.mult))
                DV.wait(dve, f"dB1.{c}")
                MM.wait(dve, f"KK1.{c}")
                if c == 0:
                    dve.wait_ge(s_retout, 80)
                halves(lambda i: f"At{i}.{c}",
                       lambda i: v.tensor_tensor(half(At, i), half(tmpF, i), quad(B[4 + i]), ALU.mult))
                MM.wait(dve, f"kT1.{c}")
                AC.wait(dve, f"kds.{c}")
                halves(lambda i: f"kdg{i}.{c}", lambda i: v.tensor_tensor(
                    half(kdg, i), quad(B[6 + i]), bc(kds[:, 4 * i:4 * i + 4], P, 2), ALU.mult))
                if c:
                    DV.did(v.tensor_tensor(beG[:, :], beta[:, c, :], eG[:, :], ALU.mult), f"beG.{c}")
                    DV.wait(dve, f"beG.{c}")
                    halves(lambda i: f"kbG{i}.{c}", lambda i: v.tensor_tensor(
                        half(kbG, i), quad(B[6 + i]), bc(beG[:, 4 * i:4 * i + 4], P, 2), ALU.mult))
                PL.wait(dve, f"Al0.{c}")
                halves(lambda i: f"U{i}.{c}", lambda i: v.scalar_tensor_tensor(
                    half(U, i), half(Al0, i), -1.0, bc(ident, 4, 1), ALU.mult, ALU.add))
                MM.wait(dve, f"QK1.{c}")
                halves(lambda i: f"attn{i}.{c}",
                       lambda i: v.tensor_tensor(half(attnT, i), quad(B[i]), half(DT, i), ALU.mult))
                MM.wait(dve, f"vT1.{c}")
                halves(lambda i: f"bv{i}.{c}", lambda i: v.tensor_tensor(
                    half(bv, i), quad(B[2 + i]), bc(beta[:, c, 4 * i:4 * i + 4], P, 2), ALU.mult))
                for lv in range(1, 7):
                    if lv < 6:
                        for i in range(2):
                            MM.wait(dve, f"dT{lv}.{i}.{c}")
                            if lv == 1:
                                AC.wait(dve, f"T{i}.{c}")
                            DV.did(v.tensor_tensor(half(T, i), half(T, i), quad(B[i]), ALU.subtract), f"T{lv}.{i}.{c}")
                    for i in range(2):
                        MM.wait(dve, f"dU{lv}.{i}.{c}")
                        DV.did(v.tensor_tensor(half(U, i), half(U, i), quad(B[2 + i]), ALU.subtract), f"U{lv}.{i}.{c}")
                    if c == 0 and lv > 1:
                        head_step(lv - 2, 2, by_head(Ps[0:NB, 0:D], RH), by_head(sqr_s[0:NB, :], RH),
                                  Ps[0:NB, 2 * D:3 * D], RH)
                    elif lv > 1:
                        head_step(lv - 2, 3, chunk_of(0, 0), chunk_of(2, 0), Pt[:, 0, Z0:Z0 + D], GH, gnw[:, :])
                if c:
                    MM.wait(dve, "qS1.1")
                    halves(lambda i: f"O{i}.{c}", lambda i: v.tensor_tensor(
                        half(tmpF, i), quad(B[2 + i]), bc(eG[:, 4 * i:4 * i + 4], P, 2), ALU.mult))
                    DV.wait(dve, "O1.1")
                    halves(lambda i: f"Oa{i}.{c}",
                           lambda i: v.tensor_tensor(half(tmpF, i), half(tmpF, i), quad(B[i]), ALU.add))
                    DV.wait(dve, "Oa1.1")
                else:
                    MM.wait(dve, "o1.0")
                    halves(lambda i: f"O{i}.{c}", lambda i: v.tensor_copy(half(chunk_of(0, 0), i), quad(B[i])))
                    DV.wait(dve, "O1.0")
                MM.wait(dve, f"dS1.{c}")
                for i in range(2):
                    if c:
                        for j in range(4):
                            h = 4 * i + j
                            t = v.scalar_tensor_tensor(Sg[:, h, :], Sg[:, h, :], eGl[:, h:h + 1],
                                                       B[4 + i][:, P * j:P * j + P], ALU.mult, ALU.add)
                    else:
                        t = v.tensor_copy(half(Sg, i), quad(B[4 + i]))
                    DV.did(t, f"S{i}.{c}")

            def gate_product(r, c, rows, sub, width, src):
                first = 512 * (r % 2) + sub
                if r < 4:
                    col = (GA0 if r < 2 else GB0) + first
                    f = Prow(c)[:, col:col + width]
                    return v.tensor_tensor(f, f, src, ALU.mult)
                f = X[rows, c, first:first + width]
                return v.tensor_tensor(f, f, src, ALU.add)

            def decoding_out(r):
                for g in range(4):
                    t = gate_product(r, 2, slice(0, NB), P * g, P, B[6 + r % 2][32 * g:32 * g + NB, 0:P])
                return t

            def mixed(r, c, rows):
                f, f2 = (Prow(c)[:, col:col + 512] for col in (GA0 + 512 * (r % 2), GB0 + 512 * (r % 2)))
                return v.tensor_tensor(f, f, f2, ALU.add)

            def branch_out(r):
                if r:
                    dve.wait_ge(s_bev, r)
                if r == 4:
                    v.memset(zrow[:, :], 0.0).then_inc(s_zr, 1)
                for c, rows in TILES:
                    dve.wait_ge(s_bt, 3 * r + c + 1)
                    if c < 2:
                        t = gate_product(r, c, slice(0, P), 0, 512, B[2 + 2 * (r % 2) + c][:, :])
                    else:
                        t = decoding_out(r)
                    if r in (2, 3):
                        link(t)
                        t = mixed(r, c, rows)
                        t.then_inc(s_mix, 1)
                        if c == 2:
                            dve.wait_ge(s_mix, 3 * r - 3)
                            dve.sem_inc(s_bev, 1)
                if r not in (2, 3):
                    t.then_inc(s_bev, 1)

            DS.did(v.memset(egd[:, :, :], 0.0), "eg")
            AS.wait(dve, "eg")
            DS.wait(dve, "eg")
            DS.did(v.tensor_tensor(egd[:, :, :], bc(gt1[0:NB, 2, :], NB, 2), bc(K[0:NB, C_ID:C_ID + NB], GH, 1),
                                   ALU.mult), "egd")
            for n, w, b0 in (("ksm", ksm, 2), ("vsm", vsm, 4)):
                MS.wait(dve, "k" if n == "ksm" else "v")
                for i in range(2):
                    t = v.tensor_copy(w[:, 512 * i:512 * i + 512], B[b0 + i][0:NB, :])
                DS.did(t, n)
            head_out(4, tmpF[:, :, :], chunk_of(2, 1), Pt[:, 1, Z0:Z0 + D], GH, gnw[:, :])
            dve.wait_ge(s_sig, 3)
            branch_out(0)
            MS.wait(dve, "kS")
            DS.wait(dve, "vsm")

            def h3(f):
                return f.rearrange("p (h n) -> p h n", h=GH)
            for h in range(GH):
                j = h % 4
                t = v.tensor_tensor(osg[0:NB, P * h:P * h + P], B[0][32 * j:32 * j + NB, P * (h // 4):P * (h // 4) + P],
                                    gt1[0:NB, 2, h:h + 1].broadcast_to([NB, P]), ALU.mult)
            DS.did(t, "vn1")
            DS.wait(dve, "vn1")
            DS.did(v.tensor_tensor(vsm[:, :], vsm[:, :], osg[0:NB, :], ALU.subtract), "vn2")
            DS.wait(dve, "vn2")
            DS.did(v.tensor_tensor(h3(vsm[:, :]), h3(vsm[:, :]), bc(beta[0:NB, 2, :], P, 2), ALU.mult), "vn3")
            dve.wait_ge(s_bt, 4)
            decoding_out(1).then_inc(s_bd, 1)
            AS.wait(dve, "egb")
            dve.wait_ge(s_sgl, 16)
            for h in range(GH):
                MS.wait(dve, f"out{h}")
                if h == 0:
                    MS.wait(dve, "kS")
                for b in range(NB):
                    t = v.scalar_tensor_tensor(Ssg[:, b, h, :], Ssg[:, b, h, :], egb[:, NB * h + b:NB * h + b + 1],
                                               B[2 + 2 * (h % 2) + b // 4][:, P * (b % 4):P * (b % 4) + P],
                                               ALU.mult, ALU.add)
                DS.did(t, f"S{h}")
            dve.wait_ge(s_bd, 1)
            for c in range(2):
                dve.wait_ge(s_bt, 5 + c)
                t = gate_product(1, c, slice(0, P), 0, 512, B[c][:, :])
            t.then_inc(s_bev, 1)
            MS.wait(dve, f"oc{GH - 1}")
            for j in range(4):
                for i in range(2):
                    f, src = osg[0:NB, 512 * i:512 * i + 512], B[6 + i][32 * j:32 * j + NB, :]
                    t = v.tensor_tensor(f, f, src, ALU.add) if j else v.tensor_copy(f, src)
                if j < 3:
                    link(t)
            DS.did(t, "osg")
            DS.wait(dve, "osg")
            sq_s = at("sq_s", ps0, [P, D])
            dve.wait_ge(s_gdnout, 16)
            head_out(5, by_head(osg[0:NB, :], GH), by_head(sq_s[0:NB, :], GH), Ps[0:NB, Z0:Z0 + D], GH, gnw[0:NB, :])

            for r in range(2, 5):
                branch_out(r)
            dve.wait_ge(s_gsout, 16 * GH)
            dve.wait_ge(s_bev, 5)
            v.memset(Lg[:, :, :], 0.0)
            v.memset(xT[:, :, :], 0.0)
            link(v.memset(xev[:, :], 1.0))
            v.tensor_copy(tw[:, :, 0:1], K[:, C_TID:C_TID + 3].unsqueeze(2))

            def norm_tile(c):
                rows = TILES[c][1]
                v.scalar_tensor_tensor(htok[0:rows, c, :], X[0:rows, c, :], rs[0:rows, c:c + 1], WN[0:rows, :],
                                       ALU.mult, ALU.mult).then_inc(s_h, 1)
            dve.wait_ge(s_wn, 32)
            dve.wait_ge(s_bt, 16)
            gate_product(5, 0, slice(0, P), 0, 512, B[4][:, :]).then_inc(s_res, 1)
            dve.wait_ge(s_rs, 2)
            link(v.reciprocal(rs[:, 0:1], rs[:, 0:1]))
            norm_tile(0)
            dve.wait_ge(s_bt, 17)
            gate_product(5, 1, slice(0, P), 0, 512, B[5][:, :]).then_inc(s_res, 1)
            dve.wait_ge(s_bt, 18)
            decoding_out(5).then_inc(s_res, 1)
            dve.wait_ge(s_rs, 3)
            link(v.reciprocal(rs[:, 1:3], rs[:, 1:3]))
            norm_tile(1)
            norm_tile(2)

            dve.wait_ge(s_lg, 3)
            for c, r in TILES:
                t = v.tensor_copy(Lg[0:r, c, :], B[2][0:r, NE * c:NE * c + NE])
            link(t)
            for c in range(3):
                t = v.max(mx[:, c, :], Lg[:, c, :])
            link(t)
            fourth = mx[:, :, TOPK - 1:TOPK].broadcast_to([P, 3, NE])
            v.tensor_tensor(ex[:, :, :], Lg[:, :, :], mx[:, :, 0:1].broadcast_to([P, 3, NE]), ALU.subtract
                            ).then_inc(s_exd, 1)
            link(v.tensor_tensor(gt[:, :, :], Lg[:, :, :], fourth, ALU.is_gt))
            link(v.tensor_tensor(eq[:, :, :], Lg[:, :, :], fourth, ALU.is_equal))
            link(v.tensor_reduce(red[:, :], gt[:, :, :], AX.X, ALU.add))
            link(v.tensor_scalar(red[:, :], red[:, :], -1.0, float(TOPK), ALU.mult, ALU.add))
            for c in range(3):
                t = v.tensor_tensor_scan(R0[:, c, :], K[:, C_ONE:C_ONE + NE], eq[:, c, :], 0.0, ALU.mult, ALU.add)
            link(t)
            link(v.tensor_tensor(R0[:, :, :], R0[:, :, :], bc(red[:, :], NE, 2), ALU.is_le))
            link(v.tensor_tensor(eq[:, :, :], eq[:, :, :], R0[:, :, :], ALU.mult))
            v.tensor_tensor(sel[:, :, :], gt[:, :, :], eq[:, :, :], ALU.add).then_inc(s_sel, 1)
            dve.wait_ge(s_sel, 1)
            dve.wait_ge(s_ex, 1)
            link(v.tensor_tensor(ex[:, :, :], ex[:, :, :], sel[:, :, :], ALU.mult))
            link(v.tensor_reduce(red[:, :], ex[:, :, :], AX.X, ALU.add))
            link(v.reciprocal(red[:, :], red[:, :]))
            link(v.tensor_tensor(Z[:, :, :], ex[:, :, :], bc(red[:, :], NE, 2), ALU.mult))
            dve.wait_ge(s_pos, 1)
            for c, r in TILES:
                t = v.scalar_tensor_tensor(R0[0:r, c, :], B[3][0:r, NE * c:NE * c + NE], 999.0, sel[0:r, c, :],
                                           ALU.add, ALU.mult)
            v.tensor_copy(cnt[:, :], B[3][0:1, 3 * NE:4 * NE])
            link(t)
            for c, r in TILES:
                for m in range(NM):
                    t = v.tensor_scalar(R[0:r, c, NE * m:NE * m + NE], R0[0:r, c, :], -1000.0 - SLOTS * m, None,
                                        ALU.add)
            t.then_inc(s_tab, 1)
            dve.wait_ge(s_tab, 1)

            def col(table, b):
                return table[:, b:b + 1] if isinstance(b, int) else table[:, bass.ds(b, 1)]

            def onehot(b, q, e):
                after(dve, m_im, 1, b)
                v.tensor_copy(tw[:, :, 1:2], Z[:, :, e:e + 1] if isinstance(e, int) else Z[:, :, bass.ds(e, 1)])
                for c, r in TILES:
                    s1 = (R[0:r, c, q:q + 1] if isinstance(q, int) else
                          R[0:r, c:c + 1, bass.ds(q, 1)].rearrange("p a n -> p (a n)"))
                    t = v.tensor_scalar(O[0:r, c, :], K[0:r, C_SLOT:C_SLOT + P], s1, None, ALU.is_equal)
                t.then_inc(m_O, 1)

            def vcol(b, i, n=1):
                return vt[:, b, i:i + n] if isinstance(b, int) else vt[:, bass.ds(b, 1), i:i + n].rearrange(
                    "p a n -> p (a n)")

            def values(b):
                after(dve, m_im, 1, b, 1)
                v.tensor_copy(vcol(b, 0, 2), B[5][:, 0:2]).then_inc(m_v, 1)

            def rows_of(b, x, y, out, steps, signal):
                v.tensor_scalar(x[:, :], vcol(b, 0), 2.0, K[:, C_DIX:C_DIX + 1], ALU.mult, ALU.add)
                v.tensor_scalar(y[:, :], vcol(b, 0), 1.0, None, ALU.min).then_inc(steps, 1)
                after(dve, steps, 2, b, 1)
                v.tensor_tensor(x[:, :], x[:, :], y[:, :], ALU.mult).then_inc(steps, 1)
                after(dve, steps, 2, b, 2)
                v.tensor_scalar(out[:, :], x[:, :], K[:, C_DIX + 1:C_DIX + 2], None, ALU.add).then_inc(signal, 1)

            def gather_rows(b):
                after(dve, m_v, 1, b, 1)
                after(dve, m_g, 16, b)
                after(dve, m_gi, 1, b)
                rows_of(b, ia, ib, gidx, m_gic, m_gi)

            def scatter_rows(b):
                after(dve, m_s, 16, b)
                after(dve, m_si, 1, b)
                rows_of(b, sa, sb_, sidx, m_sic, m_si)

            def activate(b):
                after(dve, m_gu, 1, b, 1)
                after(dve, m_act, 1, b)
                v.tensor_scalar(glu[:, :], B[0][:, :], 7.0, None, ALU.min).then_inc(m_glu, 1)
                v.tensor_scalar(lin[:, :], B[1][:, :], 7.0, -7.0, ALU.min, ALU.max).then_inc(m_gl, 1)
                after(dve, m_gl, 1, b, 1)
                after(dve, m_glu, 1, b, 1)
                v.scalar_tensor_tensor(lin[:, :], lin[:, :], 1.0, glu[:, :], ALU.add, ALU.mult).then_inc(m_lin, 1)
                after(dve, m_lin, 1, b, 1)
                after(dve, m_sig, 1, b, 1)
                after(dve, m_ta, 1, b)
                v.tensor_tensor(ac[:, :], lin[:, :], sg[:, :], ALU.mult).then_inc(m_act, 1)

            for b in range(3):
                onehot(b, b, b)
                if b == 2:
                    activate(0)
                values(b)
                gather_rows(b)
            def step(b):
                onehot(b + 2, b + 2, b + 2)
                scatter_rows(b - 1)
                activate(b)
                values(b + 2)
                gather_rows(b + 2)

            step(1)
            for m in range(1, NM):
                v.tensor_scalar(xval[:, NE * (m - 1):NE * m], cnt[:, :], float(SLOTS * m), None, ALU.is_gt)
                t = v.tensor_scalar(xtmp[:, m - 1, 0:NE], K[0:1, C_QV:C_QV + NE], -float(NE), None, ALU.add)
            link(t)
            link(v.tensor_tensor_scan(xpre[:, :], xev[:, :], xval[:, :], 0.0, ALU.mult, ALU.add))
            v.tensor_copy(xni[:, :], xpre[:, NX - 1:NX])
            link(v.tensor_copy(xev[:, :].rearrange("p (m e) -> p m e", e=NE), xtmp[:, 0:NM - 1, 0:NE]))
            link(v.tensor_tensor(xcmp[:, :, :], bc(xpre[:, :], NEXTRA, 1), bc(K[0:1, C_J:C_J + NEXTRA], NX, 2),
                                 ALU.is_equal))
            link(v.tensor_tensor(xcmp[:, :, :], xcmp[:, :, :], bc(xval[:, :], NEXTRA, 1), ALU.mult))
            for table, floats, ints in ((K[0:1, C_QV:C_QV + NX], xql, xqi), (xev[:, :], xel, xei)):
                link(v.tensor_tensor(xtmp[:, :, :], xcmp[:, :, :], bc(table, NEXTRA, 1), ALU.mult))
                link(v.tensor_reduce(floats[:, :], xtmp[:, :, :], AX.X, ALU.add))
                v.tensor_copy(ints[:, :], floats[:, :]).then_inc(s_ext, 1)
            with dve.Fori(2, NE - 2) as b:
                step(b)
            scatter_rows(NE - 3)
            activate(NE - 2)
            scatter_rows(NE - 2)
            activate(NE - 1)
            scatter_rows(NE - 1)

            def extra(j, b):
                q = dve.value_load(xqi[0:1, bass.ds(j, 1)], min_val=NE, max_val=NE * NM - 1)
                e = dve.value_load(xei[0:1, bass.ds(j, 1)], min_val=0, max_val=NE - 1)
                onehot(b, q, e)
                values(b)
                gather_rows(b)
                activate(b)
                scatter_rows(b)
            extra_blocks(dve, extra)
            normed(2)


_INS = ["x_prompt", "x_sample", "state_ret", "state_gdn", "state_conv", "attn_norm_w", "w_in", "conv_w", "a_log",
        "dt_bias", "gdn_norm_w", "w_branch_a", "w_branch_b", "w_out", "ffn_norm_w", "w_router", "b_router",
        "w_gate_up", "b_gate_up", "w_down", "b_down", "final_norm_w"]
_OUTS = [(1, 256, 1024), (8, 1, 1024), (1, 1, 4, 128, 256), (1, 1, 8, 128, 128), (1, 1, 3, 3072),
         (1, 8, 4, 128, 256), (1, 8, 8, 128, 128), (1, 8, 3, 3072)]


def kernel(**inputs):
    import concourse.bacc as bacc
    from concourse.bass_utils import run_bass_kernel_spmd

    nc = bacc.Bacc("TRN2", target_bir_lowering=False, num_devices=1)
    arrays, d, outs = {}, {}, []
    for name in _INS + ["consts"]:
        a = np.ascontiguousarray(constants() if name == "consts" else inputs[name])
        arrays[f"in_{name}"] = a
        d[name] = nc.dram_tensor(f"in_{name}", a.shape, mybir.dt.from_np(a.dtype), kind="ExternalInput").ap()
    for i, shape in enumerate(_OUTS):
        outs.append(nc.dram_tensor(f"out_{i}", shape, F32, kind="ExternalOutput").ap())
    build_layer(nc, d, outs)
    r = run_bass_kernel_spmd(nc, [arrays], core_ids=[0])
    return tuple(r.results[0][f"out_{i}"] for i in range(len(_OUTS)))
```
